# Optimizing a Trainium2 kernel written in Bass

```python
import jax, jax.numpy as jnp
from jax import lax
import numpy as np
import math

D_MODEL = 1024
BATCH = 1
SEQ = 2048
DEPTH = 1

HEAD_DIM = 64
MIX_WIDTH = D_MODEL
FOX_HEADS = (MIX_WIDTH // 2) // HEAD_DIM
SWA_Q_HEADS = (MIX_WIDTH // 2) // HEAD_DIM
SWA_KV_HEADS = 2
SWA_GROUP = SWA_Q_HEADS // SWA_KV_HEADS
WINDOW = 128
Q_BLOCK = 128
ROPE_THETA = 10000.0
RMS_EPS = 1e-6
FOX_W = FOX_HEADS * HEAD_DIM
SWA_W = SWA_Q_HEADS * HEAD_DIM
SWA_KV_W = SWA_KV_HEADS * HEAD_DIM
IN_SIZES = (FOX_W, FOX_W, FOX_W, FOX_HEADS, FOX_W, SWA_W, SWA_KV_W, SWA_KV_W, SWA_W)
IN_WIDTH = FOX_W * 4 + FOX_HEADS + SWA_W * 2 + SWA_KV_W * 2


def rms_norm(x, g):
    xf = x.astype(jnp.float32)
    y = xf * lax.rsqrt(jnp.mean(xf * xf, axis=-1, keepdims=True) + RMS_EPS)
    return (y * g.astype(jnp.float32)).astype(x.dtype)

def rope(x, positions):
    half = HEAD_DIM // 2
    inv_freq = ROPE_THETA ** (-jnp.arange(half, dtype=jnp.float32) / half)
    ang = positions.astype(jnp.float32)[..., None] * inv_freq
    cos = jnp.cos(ang)[:, :, None, :]
    sin = jnp.sin(ang)[:, :, None, :]
    xf = x.astype(jnp.float32)
    x1, x2 = xf[..., :half], xf[..., half:]
    return jnp.concatenate([x1 * cos - x2 * sin, x2 * cos + x1 * sin], axis=-1).astype(x.dtype)

def forgetting_attention(q, k, v, f_logit):
    B, S, H, d = q.shape
    nb = S // Q_BLOCK
    cum = jnp.cumsum(jax.nn.log_sigmoid(f_logit.astype(jnp.float32)), axis=1)
    cum = cum.transpose(0, 2, 1)
    kh = k.transpose(0, 2, 1, 3)
    vh = v.transpose(0, 2, 1, 3)
    q_blocks = q.transpose(0, 2, 1, 3).reshape(B, H, nb, Q_BLOCK, d).transpose(2, 0, 1, 3, 4)
    c_blocks = cum.reshape(B, H, nb, Q_BLOCK).transpose(2, 0, 1, 3)
    key_pos = jnp.arange(S)
    scale = d ** -0.5

    def one_block(args):
        qb, cb, n = args
        s = jnp.einsum('bhqd,bhkd->bhqk', qb, kh, preferred_element_type=jnp.float32) * scale
        s = s + cb[..., None] - cum[:, :, None, :]
        q_pos = n * Q_BLOCK + jnp.arange(Q_BLOCK)
        causal = key_pos[None, :] <= q_pos[:, None]
        s = jnp.where(causal, s, -jnp.inf)
        p = jax.nn.softmax(s, axis=-1)
        return jnp.einsum('bhqk,bhkd->bhqd', p.astype(vh.dtype), vh)

    out = lax.map(one_block, (q_blocks, c_blocks, jnp.arange(nb)))
    return out.transpose(1, 0, 3, 2, 4).reshape(B, S, H * d)

def sliding_window_sink_attention(q, k, v, sinks):
    B, S, _, d = q.shape
    nb = S // Q_BLOCK
    qb = q.reshape(B, nb, Q_BLOCK, SWA_KV_HEADS, SWA_GROUP, d)

    def with_prev(t):
        t = t.reshape(B, nb, Q_BLOCK, SWA_KV_HEADS, d)
        prev = jnp.pad(t[:, :-1], ((0, 0), (1, 0), (0, 0), (0, 0), (0, 0)))
        return jnp.concatenate([prev, t], axis=2)

    kk, vv = with_prev(k), with_prev(v)
    s = jnp.einsum('bnqhgd,bnshd->bnhgqs', qb, kk, preferred_element_type=jnp.float32) * (d ** -0.5)
    i = jnp.arange(Q_BLOCK)[:, None]
    j = jnp.arange(2 * Q_BLOCK)[None, :]
    rel = i + Q_BLOCK - j
    band = (rel >= 0) & (rel < WINDOW)
    valid_blk = (jnp.arange(nb)[:, None, None] > 0) | (j[None] >= Q_BLOCK)
    mask = band[None] & valid_blk
    s = jnp.where(mask[None, :, None, None], s, -jnp.inf)
    sink = jnp.broadcast_to(
        sinks.astype(jnp.float32).reshape(SWA_KV_HEADS, SWA_GROUP)[None, None, :, :, None, None],
        s.shape[:-1] + (1,))
    p = jax.nn.softmax(jnp.concatenate([s, sink], axis=-1), axis=-1)[..., :-1]
    out = jnp.einsum('bnhgqs,bnshd->bnqhgd', p.astype(vv.dtype), vv)
    return out.reshape(B, S, SWA_Q_HEADS * d)

def first_inputs(seed: int = 0) -> dict:
    key = jax.random.key(seed)
    ks = jax.random.split(key, 12)
    x = jax.random.normal(ks[0], (BATCH, SEQ, D_MODEL), jnp.float32)
    c = jax.random.normal(ks[1], (BATCH, D_MODEL), jnp.float32)
    positions = jnp.broadcast_to(jnp.arange(SEQ, dtype=jnp.int32)[None, :], (BATCH, SEQ))
    w_ada = jax.random.normal(ks[2], (DEPTH, D_MODEL, 3 * D_MODEL), jnp.float32) * (0.5 * D_MODEL ** -0.5)
    b_ada = jax.random.normal(ks[3], (DEPTH, 3 * D_MODEL), jnp.float32) * 0.02
    g_pre = 1.0 + 0.1 * jax.random.normal(ks[4], (DEPTH, D_MODEL), jnp.float32)
    w_in = jax.random.normal(ks[5], (DEPTH, D_MODEL, IN_WIDTH), jnp.float32) * D_MODEL ** -0.5
    b_fgate = jax.random.uniform(ks[6], (DEPTH, FOX_HEADS), jnp.float32, 1.0, 4.0)
    sinks = jax.random.normal(ks[7], (DEPTH, SWA_Q_HEADS), jnp.float32)
    w_out = jax.random.normal(ks[8], (DEPTH, MIX_WIDTH, D_MODEL), jnp.float32) * MIX_WIDTH ** -0.5
    g_post = 1.0 + 0.1 * jax.random.normal(ks[9], (DEPTH, D_MODEL), jnp.float32)
    return {"x": x, "c": c, "positions": positions, "w_ada": w_ada, "b_ada": b_ada,
            "g_pre": g_pre, "w_in": w_in, "b_fgate": b_fgate, "sinks": sinks,
            "w_out": w_out, "g_post": g_post}

def first_block(x, c, positions, w_ada, b_ada, g_pre, w_in, b_fgate, sinks, w_out, g_post):
    B, S, _ = x.shape
    split_points = [int(v) for v in np.cumsum(IN_SIZES)[:-1]]
    for l in range(DEPTH):
        mod = jax.nn.silu(c) @ w_ada[l] + b_ada[l]
        shift, scale, gate = jnp.split(mod, 3, axis=-1)
        h = rms_norm(x, g_pre[l]) * (1.0 + scale[:, None, :]) + shift[:, None, :]
        proj = h @ w_in[l]
        qa, ka, va, fa, za, qb, kb, vb, zb = jnp.split(proj, split_points, axis=-1)
        oa = forgetting_attention(
            qa.reshape(B, S, FOX_HEADS, HEAD_DIM),
            ka.reshape(B, S, FOX_HEADS, HEAD_DIM),
            va.reshape(B, S, FOX_HEADS, HEAD_DIM),
            fa + b_fgate[l])
        oa = oa * jax.nn.silu(za)
        qb = rope(qb.reshape(B, S, SWA_Q_HEADS, HEAD_DIM), positions)
        kb = rope(kb.reshape(B, S, SWA_KV_HEADS, HEAD_DIM), positions)
        ob = sliding_window_sink_attention(qb, kb, vb.reshape(B, S, SWA_KV_HEADS, HEAD_DIM), sinks[l])
        ob = ob * jax.nn.silu(zb)
        y = jnp.concatenate([oa, ob], axis=-1) @ w_out[l]
        x = x + gate[:, None, :] * rms_norm(y, g_post[l])
    return x


N_META = 16
MIX_WIDTH_2 = D_MODEL
ATTN_WIDTH = MIX_WIDTH_2 // 2
HGRN_WIDTH = MIX_WIDTH_2 - ATTN_WIDTH
ATTN_HEADS = 8
ATTN_HEAD_DIM = ATTN_WIDTH // ATTN_HEADS
KV_RANK = 128
IDX_HEADS = 4
IDX_DIM = 64
TOPK_MAX = 256
HGRN_EXPAND = 128
HGRN_HEADS = HGRN_WIDTH // HGRN_EXPAND
HGRN_CHUNK = 64
REL_BUCKETS = 32
REL_MAX_DIST = 128
DN_ALPHA = (2 * DEPTH) ** 0.25
DN_BETA = (8 * DEPTH) ** -0.25
EPS = 1e-6

IN_SIZES_2 = (ATTN_WIDTH, KV_RANK, IDX_HEADS * IDX_DIM, IDX_DIM, IDX_HEADS, ATTN_WIDTH,
            HGRN_WIDTH, HGRN_WIDTH, HGRN_WIDTH, HGRN_WIDTH)
N_IN = sum(IN_SIZES_2)
IN_OFFSETS = tuple(int(v) for v in np.cumsum(IN_SIZES_2)[:-1])


def layer_norm(x, g, b):
    xf = x.astype(jnp.float32)
    mu = jnp.mean(xf, axis=-1, keepdims=True)
    var = jnp.mean(jnp.square(xf - mu), axis=-1, keepdims=True)
    return ((xf - mu) * lax.rsqrt(var + EPS) * g + b).astype(x.dtype)

def rms_norm_2(x, g):
    xf = x.astype(jnp.float32)
    return (xf * lax.rsqrt(jnp.mean(jnp.square(xf), axis=-1, keepdims=True) + EPS) * g).astype(x.dtype)

def t5_bucket(dist):
    n = jnp.maximum(dist, 0)
    max_exact = REL_BUCKETS // 2
    nf = jnp.maximum(n, 1).astype(jnp.float32)
    large = max_exact + (jnp.log(nf / max_exact) / math.log(REL_MAX_DIST / max_exact)
                         * (REL_BUCKETS - max_exact)).astype(jnp.int32)
    large = jnp.minimum(large, REL_BUCKETS - 1)
    return jnp.where(n < max_exact, n, large)

def dsa_attention(q, c, qi, ki, wi, rel_bias, w_uk, w_uv):
    B, E = c.shape[0], c.shape[1]
    S = E - N_META
    k_top = min(TOPK_MAX, S // 4)
    scale = ATTN_HEAD_DIM ** -0.5
    q_lat = jnp.einsum('bthd,hdc->bthc', q, w_uk)
    c_m, c_r = c[:, :N_META], c[:, N_META:]
    ql_m, ql_r = q_lat[:, :N_META], q_lat[:, N_META:]
    qi_r, ki_r = qi[:, N_META:], ki[:, N_META:]
    wi_r = wi[:, N_META:] * (IDX_HEADS ** -0.5)
    meta_pos = jnp.arange(N_META)
    key_pos = jnp.arange(S)
    b_idx = jnp.arange(B)[:, None, None]

    lg = jnp.einsum('bqhc,bmc->bqhm', ql_m, c_m).astype(jnp.float32) * scale
    bm = rel_bias[t5_bucket(meta_pos[:, None] - meta_pos[None, :])]
    lg = lg + jnp.transpose(bm, (0, 2, 1))[None].astype(jnp.float32)
    lg = jnp.where((meta_pos[:, None] >= meta_pos[None, :])[None, :, None, :], lg, -jnp.inf)
    o_m = jnp.einsum('bqhm,bmc->bqhc', jax.nn.softmax(lg, axis=-1).astype(c.dtype), c_m)

    def block(bi):
        start = bi * Q_BLOCK
        q_pos = start + jnp.arange(Q_BLOCK)
        ql = lax.dynamic_slice_in_dim(ql_r, start, Q_BLOCK, axis=1)
        qib = lax.dynamic_slice_in_dim(qi_r, start, Q_BLOCK, axis=1)
        wib = lax.dynamic_slice_in_dim(wi_r, start, Q_BLOCK, axis=1)
        s_h = jax.nn.relu(jnp.einsum('bqhd,bkd->bqhk', qib, ki_r).astype(jnp.float32) * (IDX_DIM ** -0.5))
        s_idx = jnp.einsum('bqhk,bqh->bqk', s_h, wib.astype(jnp.float32))
        causal = key_pos[None, :] <= q_pos[:, None]
        s_idx = jnp.where(causal[None], s_idx, -jnp.inf)
        _, sel = lax.top_k(s_idx, k_top)
        valid = sel <= q_pos[None, :, None]
        c_sel = c_r[b_idx, sel]
        lg_s = jnp.einsum('bqhc,bqkc->bqhk', ql, c_sel).astype(jnp.float32) * scale
        bs = rel_bias[t5_bucket(q_pos[None, :, None] - sel)]
        lg_s = lg_s + jnp.moveaxis(bs, -1, 2).astype(jnp.float32)
        lg_s = jnp.where(valid[:, :, None, :], lg_s, -jnp.inf)
        lg_m = jnp.einsum('bqhc,bmc->bqhm', ql, c_m).astype(jnp.float32) * scale
        bmr = rel_bias[t5_bucket(N_META + q_pos[:, None] - meta_pos[None, :])]
        lg_m = lg_m + jnp.transpose(bmr, (0, 2, 1))[None].astype(jnp.float32)
        p = jax.nn.softmax(jnp.concatenate([lg_m, lg_s], axis=-1), axis=-1).astype(c.dtype)
        return (jnp.einsum('bqhm,bmc->bqhc', p[..., :N_META], c_m)
                + jnp.einsum('bqhk,bqkc->bqhc', p[..., N_META:], c_sel))

    o_r = lax.map(block, jnp.arange(S // Q_BLOCK))
    o_r = jnp.moveaxis(o_r, 0, 1).reshape(B, S, ATTN_HEADS, KV_RANK)
    o_lat = jnp.concatenate([o_m, o_r], axis=1)
    return jnp.einsum('bthc,hcd->bthd', o_lat, w_uv).reshape(B, E, ATTN_WIDTH)

def hgrn2(q, f_raw, i, lb):
    B, E = q.shape[0], q.shape[1]
    dt = q.dtype
    qf = jax.nn.silu(q.astype(jnp.float32)) * (HGRN_EXPAND ** -0.5)
    f = lb + (1.0 - lb) * jax.nn.sigmoid(f_raw.astype(jnp.float32))
    g = jnp.log(f)
    k = 1.0 - f
    v = i.astype(jnp.float32)
    pad = HGRN_CHUNK - N_META

    def to_chunks(a):
        a = jnp.pad(a, ((0, 0), (pad, 0), (0, 0)))
        n = a.shape[1] // HGRN_CHUNK
        return a.reshape(B, n, HGRN_CHUNK, HGRN_HEADS, HGRN_EXPAND).transpose(1, 0, 3, 2, 4)

    tri = jnp.tril(jnp.ones((HGRN_CHUNK, HGRN_CHUNK), dtype=bool))

    def step(state, inp):
        qc, kc, vc, gc = inp
        bcum = jnp.cumsum(gc, axis=2)
        o_inter = jnp.einsum('bhtk,bhkv->bhtv', qc * jnp.exp(bcum), state)
        diff = bcum[:, :, :, None, :] - bcum[:, :, None, :, :]
        decay = jnp.exp(jnp.where(tri[:, :, None], diff, -jnp.inf))
        scores = jnp.sum(qc[:, :, :, None, :] * decay * kc[:, :, None, :, :], axis=-1)
        o_intra = jnp.einsum('bhts,bhsv->bhtv', scores, vc)
        b_last = bcum[:, :, -1:, :]
        new_state = (jnp.exp(b_last[:, :, 0, :])[..., None] * state
                     + jnp.einsum('bhsk,bhsv->bhkv', kc * jnp.exp(b_last - bcum), vc))
        return new_state, o_inter + o_intra

    s0 = jnp.zeros((B, HGRN_HEADS, HGRN_EXPAND, HGRN_EXPAND), jnp.float32)
    _, outs = lax.scan(step, s0, (to_chunks(qf), to_chunks(k), to_chunks(v), to_chunks(g)))
    n = outs.shape[0]
    o = outs.transpose(1, 0, 3, 2, 4).reshape(B, n * HGRN_CHUNK, HGRN_HEADS, HGRN_EXPAND)[:, pad:]
    return o.astype(dt)

def second_inputs(seed: int = 0) -> dict:
    key = jax.random.key(seed)
    ks = jax.random.split(key, 12)
    nrm = jax.random.normal
    x = nrm(ks[0], (BATCH, SEQ, D_MODEL), jnp.float32)
    meta_tokens = nrm(ks[1], (N_META, D_MODEL), jnp.float32)
    rel_bias = 0.5 * nrm(ks[2], (REL_BUCKETS, ATTN_HEADS), jnp.float32)
    hgrn_lb_raw = nrm(ks[3], (DEPTH, HGRN_WIDTH), jnp.float32)
    w_in = nrm(ks[4], (DEPTH, D_MODEL, N_IN), jnp.float32) * D_MODEL ** -0.5
    kv_norm_g = 1.0 + 0.1 * nrm(ks[5], (DEPTH, KV_RANK), jnp.float32)
    w_uk = nrm(ks[6], (DEPTH, ATTN_HEADS, ATTN_HEAD_DIM, KV_RANK), jnp.float32) * ATTN_HEAD_DIM ** -0.5
    w_uv = nrm(ks[7], (DEPTH, ATTN_HEADS, KV_RANK, ATTN_HEAD_DIM), jnp.float32) * (KV_RANK ** -0.5 * DN_BETA)
    hgrn_norm_g = 1.0 + 0.1 * nrm(ks[8], (DEPTH, HGRN_EXPAND), jnp.float32)
    w_out = nrm(ks[9], (DEPTH, MIX_WIDTH_2, D_MODEL), jnp.float32) * (MIX_WIDTH_2 ** -0.5 * DN_BETA)
    ln_g = 1.0 + 0.1 * nrm(ks[10], (DEPTH, D_MODEL), jnp.float32)
    ln_b = 0.02 * nrm(ks[11], (DEPTH, D_MODEL), jnp.float32)
    return {"x": x, "meta_tokens": meta_tokens, "rel_bias": rel_bias, "hgrn_lb_raw": hgrn_lb_raw,
            "w_in": w_in, "kv_norm_g": kv_norm_g, "w_uk": w_uk, "w_uv": w_uv,
            "hgrn_norm_g": hgrn_norm_g, "w_out": w_out, "ln_g": ln_g, "ln_b": ln_b}

def second_block(x, meta_tokens, rel_bias, hgrn_lb_raw, w_in, kv_norm_g, w_uk, w_uv,
              hgrn_norm_g, w_out, ln_g, ln_b):
    B = x.shape[0]
    h = jnp.concatenate([jnp.broadcast_to(meta_tokens[None].astype(x.dtype), (B, N_META, D_MODEL)), x], axis=1)
    E = h.shape[1]
    lb_p = jax.nn.softmax(hgrn_lb_raw.astype(jnp.float32), axis=0)
    lb_all = jnp.cumsum(lb_p, axis=0) - lb_p[0:1]
    for l in range(DEPTH):
        proj = h @ w_in[l]
        (q_a, c_kv, q_idx, k_idx, w_idx, gate_a,
         q_h, f_h, i_h, gate_h) = jnp.split(proj, IN_OFFSETS, axis=-1)
        a = dsa_attention(q_a.reshape(B, E, ATTN_HEADS, ATTN_HEAD_DIM), rms_norm_2(c_kv, kv_norm_g[l]),
                          q_idx.reshape(B, E, IDX_HEADS, IDX_DIM), k_idx, w_idx,
                          rel_bias, w_uk[l], w_uv[l])
        a = a * jax.nn.silu(gate_a)
        r = hgrn2(q_h, f_h, i_h, lb_all[l])
        r = rms_norm_2(r, hgrn_norm_g[l]).reshape(B, E, HGRN_WIDTH) * jax.nn.silu(gate_h)
        y = jnp.concatenate([a, r], axis=-1) @ w_out[l]
        h = layer_norm(DN_ALPHA * h + y, ln_g[l], ln_b[l])
    return h[:, N_META:]


def setup_inputs(seed=0):
    out = dict(first_inputs(seed))
    for name, value in second_inputs(seed + 1).items():
        if name != "x":
            out[name + "_2"] = value
    return out


def reference(
    x, c, positions, w_ada, b_ada, g_pre, w_in, b_fgate, sinks, w_out, g_post, meta_tokens_2,
    rel_bias_2, hgrn_lb_raw_2, w_in_2, kv_norm_g_2, w_uk_2, w_uv_2, hgrn_norm_g_2, w_out_2,
    ln_g_2, ln_b_2,
):
    x = first_block(
        x, c, positions, w_ada, b_ada, g_pre, w_in, b_fgate, sinks, w_out, g_post,
    )
    return second_block(
        x, meta_tokens_2, rel_bias_2, hgrn_lb_raw_2, w_in_2, kv_norm_g_2, w_uk_2, w_uv_2,
        hgrn_norm_g_2, w_out_2, ln_g_2, ln_b_2,
    )


_drawn_inputs = setup_inputs


def setup_inputs(seed=0):
    import zlib

    import numpy as np

    out = dict(_drawn_inputs(seed))
    spreads = {}
    factors = {'sinks': 8.0,
     'meta_tokens_2': 6.66,
     'rel_bias_2': 8.0,
     'kv_norm_g_2': 8.0,
     'hgrn_norm_g_2': 2.851,
     'ln_b_2': 2.676}
    for name, (base, spread) in spreads.items():
        noise = np.random.default_rng([zlib.crc32(name.encode()), seed]).standard_normal(out[name].shape)
        drawn = base * np.exp(spread * noise) if base else spread * noise
        out[name] = __import__('jax').numpy.asarray(drawn.astype(out[name].dtype))
    for name, factor in factors.items():
        out[name] = (out[name] * factor).astype(out[name].dtype)
    return out
```

```python
import numpy as np
from contextlib import ExitStack
import concourse.bass as bass
from concourse import mybir

F32 = mybir.dt.float32
F32R = mybir.dt.float32r
BF16 = mybir.dt.bfloat16
I32 = mybir.dt.int32
ALU = mybir.AluOpType
ACT = mybir.ActivationFunctionType
AX = mybir.AxisListType
ds = bass.ds

P = 128
S = 2048
D = 1024
NT = S // P
DC = D // P
NMETA = 16
E = NMETA + S
NEG = -1.0e30


class Tally:

    def __init__(self, eng, sem):
        self.eng, self.sem, self.at, self.lap, self.base = eng, sem, 0, 0, 0

    def up(self, ins):
        ins.then_inc(self.sem, 1)
        self.at += 1
        return ins

    def settle(self):
        self.eng.wait_ge(self.sem, self.lap + self.at)

    def enter(self, i, per):
        self.base, self.per, self.lap = self.at, per, i * per

    def leave(self, laps):
        assert self.at - self.base == self.per, (self.at - self.base, self.per)
        self.lap = 0
        self.at = self.base + self.per * laps


class Memory:

    def __init__(self, nc, own, used):
        self.nc, self.own, self.used = nc, own, used

    def sb(self, name, shape, dt=F32):
        return self.own.enter_context(self.nc.sbuf_tensor(name, shape, dt))

    def ps(self, name, shape, dt=F32):
        return self.own.enter_context(self.nc.psum_tensor(name, shape, dt))

    def sem(self, name):
        self.used.append(self.nc.alloc_semaphore(name=name))
        return self.used[-1]


def clear(nc, used):
    nc.clear_and_free_semaphores(used)
    nc.all_engine_barrier()
    used.clear()


def cols(v, n):
    return v.rearrange("a (k p) -> p (a k)", p=P)



def stage_modulate(nc, used, x, c, w_ada, b_ada, g_pre, g_post, hT, gate_row):
    hT_hi, hT_lo = hT
    HALF = 12
    with ExitStack() as own:
        m = Memory(nc, own, used)
        wa = m.sb("wa", [P, 2, HALF * P])
        c_col, c_sig, c_act = (m.sb(n, [P, DC]) for n in ("c_col", "c_sig", "c_act"))
        b_col = m.sb("b_col", [P, 3 * DC])
        mod = m.sb("mod", [P, 3 * DC])
        gpre_col, gpost_col, gain, gated = (m.sb(n, [P, DC]) for n in ("gpre", "gpost", "gain", "gated"))
        ident = m.sb("identA", [P, P])
        ones = m.sb("onesA", [P, P])
        diag = m.sb("diag", [P, DC, P])
        xt = m.sb("xt", [P, 4, D])
        xn = m.sb("xn", [P, 2, D])
        junk = m.sb("junkA", [P, D])
        ssq, var, std, rstd = (m.sb(n, [P, NT]) for n in ("ssq", "var", "std", "rstd"))
        full = m.sb("fullA", [P, 2, DC, P])
        pmod = m.ps("pmod", [P, 512])
        prow = m.ps("prow", [P, D])
        pT = m.ps("pTA", [P, 2, D])

        s_vec = m.sem("a_vectors_loaded")
        s_w = [m.sem(f"a_w_ada_loaded{i}") for i in range(2)]
        s_x = [m.sem(f"a_x_loaded{i}") for i in range(4)]
        s_const = m.sem("a_constants_made")
        s_sig = m.sem("a_sigmoid_of_c")
        s_cact = m.sem("a_silu_of_c")
        s_wused = m.sem("a_w_ada_used")
        s_gated = m.sem("a_gate_diagonals")
        s_prow = m.sem("a_gate_row_in_psum")
        s_ssq = m.sem("a_sum_of_squares")
        s_var = m.sem("a_mean_square")
        s_std = m.sem("a_root")
        s_rstd = m.sem("a_rstd")
        s_xn = m.sem("a_rows_normalised")
        s_tr = m.sem("a_rows_transposed")
        s_full = m.sem("a_modulated")
        s_hi = m.sem("a_high_part")
        s_lo = m.sem("a_low_part")
        s_dve = m.sem("a_dve_own")
        s_gp = m.sem("a_pool_own")

        def skeleton(eng, phases, tally=None, per=0):
            def turns(ts):
                for t in ts:
                    for off, phase in phases:
                        if 0 <= t + off < NT:
                            phase(t + off, (t + off) % 4, (t + off) // 4)
            turns(range(-2, 1))
            laps = (NT - 4) // 4
            with eng.Fori(0, laps) as i:
                if tally:
                    tally.enter(i, per)
                for j in range(1, 5):
                    for off, phase in phases:
                        phase(i * 4 + (j + off), (j + off) % 4, i + (j + off) // 4)
                if tally:
                    tally.leave(laps)
            turns(range(NT - 3, NT + 1))

        block = own.enter_context(nc.Block())

        @block.sync
        def _(sp):
            with nc.allow_non_contiguous_dma(reason="vectors of a few KB, once"):
                sp.dma_start(c_col[:], cols(c, DC)).then_inc(s_vec, 16)
                sp.dma_start(b_col[:], cols(b_ada, 3 * DC)).then_inc(s_vec, 16)
                sp.dma_start(gpre_col[:], cols(g_pre, DC)).then_inc(s_vec, 16)
                sp.dma_start(gpost_col[:], cols(g_post, DC)).then_inc(s_vec, 16)
            for k in range(DC):
                for j in range(2):
                    n = 2 * k + j
                    if n >= 2:
                        sp.wait_ge(s_wused, n - 1)
                    sp.dma_start(wa[:, j, :], w_ada[0, k * P:(k + 1) * P, j * HALF * P:(j + 1) * HALF * P]
                                 ).then_inc(s_w[j], 16)

        @block.gpsimd
        def _(gp):
            own_ = Tally(gp, s_gp)
            own_.up(gp.memset(ident[:], 0.0))
            own_.up(gp.memset(ones[:], 1.0))
            own_.settle()
            gp.affine_select(out=ident[:], in_=ident[:], compare_op=ALU.not_equal, fill=1.0, base=0,
                             pattern=[[-1, P]], channel_multiplier=1).then_inc(s_const, 1)
            for t in range(4):
                gp.dma_start(xt[:, t, :], x[t * P:(t + 1) * P, :]).then_inc(s_x[t], 16)
            with gp.Fori(0, (NT - 4) // 4) as i:
                for j in range(4):
                    gp.wait_ge(s_xn, i * 4 + j + 1)
                    gp.dma_start(xt[:, j, :], x[ds(i * (4 * P) + (4 + j) * P, P), :]).then_inc(s_x[j], 16)

        @block.scalar
        def _(act):
            act.wait_ge(s_vec, 64)
            act.activation(c_sig[:], c_col[:], ACT.Sigmoid).then_inc(s_sig, 1)

            def root(t, j, r):
                act.wait_ge(s_x[j], r * 16 + 16)
                act.activation(junk[:], xt[:, j, :], ACT.Square, accum_out=ssq[:, ds(t, 1)]).then_inc(s_ssq, 1)
                act.wait_ge(s_var, t + 1)
                act.activation(std[:, ds(t, 1)], var[:, ds(t, 1)], ACT.Sqrt).then_inc(s_std, 1)

            def high(t, j, r):
                act.wait_ge(s_full, t + 1)
                act.activation(hT_hi[:, :, ds(t * P, P)], full[:, j % 2, :, :], ACT.Copy).then_inc(s_hi, 1)
            skeleton(act, ((0, high), (2, root)))

        @block.vector
        def _(v):
            own_ = Tally(v, s_dve)
            v.wait_ge(s_sig, 1)
            v.tensor_tensor(c_act[:], c_sig[:], c_col[:], ALU.mult).then_inc(s_cact, 1)
            v.wait_ge(s_wused, 2 * DC)
            own_.up(v.tensor_tensor(mod[:], pmod[:, 0:3 * DC], b_col[:], ALU.add))
            own_.settle()
            own_.up(v.scalar_tensor_tensor(gain[:], mod[:, DC:2 * DC], 1.0, gpre_col[:], ALU.add, ALU.mult))
            own_.up(v.tensor_tensor(gated[:], mod[:, 2 * DC:], gpost_col[:], ALU.mult))
            own_.settle()
            v.wait_ge(s_const, 1)
            for k in range(DC):
                last = v.tensor_scalar(diag[:, k, :], ident[:], gated[:, k:k + 1], None, ALU.mult)
            last.then_inc(s_gated, 1)
            v.wait_ge(s_prow, 1)
            own_.up(v.tensor_copy(gate_row[:], prow[:]))

            def variance(t, j, r):
                v.wait_ge(s_ssq, t + 1)
                v.tensor_scalar(var[:, ds(t, 1)], ssq[:, ds(t, 1)], 1.0 / D, 1e-6, ALU.mult, ALU.add
                                ).then_inc(s_var, 1)

            def normalise(t, j, r):
                v.wait_ge(s_std, t + 1)
                own_.up(v.reciprocal(rstd[:, ds(t, 1)], std[:, ds(t, 1)]))
                own_.settle()
                v.tensor_scalar(xn[:, j % 2, :], xt[:, j, :], rstd[:, ds(t, 1)], None, ALU.mult).then_inc(s_xn, 1)

            def modulate(t, j, r):
                v.wait_ge(s_tr, t + 1)
                if not isinstance(t, int) or t >= 2:
                    v.wait_ge(s_lo, t - 1)
                for k in range(DC):
                    last = v.tensor_scalar(full[:, j % 2, k, :], pT[:, j % 2, k * P:(k + 1) * P],
                                           gain[:, k:k + 1], mod[:, k:k + 1], ALU.mult, ALU.add)
                last.then_inc(s_full, 1)

            def low(t, j, r):
                v.wait_ge(s_hi, t + 1)
                v.tensor_tensor(hT_lo[:, :, ds(t * P, P)], full[:, j % 2, :, :],
                                hT_hi[:, :, ds(t * P, P)].bitcast(F32), ALU.subtract).then_inc(s_lo, 1)
            skeleton(v, ((1, normalise), (0, modulate), (-1, low), (2, variance)), own_, 4)

        @block.tensor
        def _(pe):
            pe.wait_ge(s_cact, 1)
            for k in range(DC):
                for j in range(2):
                    pe.wait_ge(s_w[j], 16 * (k + 1))
                    for q in range(HALF):
                        col = j * HALF + q
                        last = pe.matmul(pmod[:, col:col + 1], lhsT=wa[:, j, q * P:(q + 1) * P],
                                         rhs=c_act[:, k:k + 1], start=(k == 0 and col == 0),
                                         stop=(k == DC - 1), skip_group_check=True)
                    last.then_inc(s_wused, 1)
            pe.wait_ge(s_gated, 1)
            for k in range(DC):
                last = pe.matmul(prow[:, k * P:(k + 1) * P], lhsT=ones[:], rhs=diag[:, k, :],
                                 start=True, stop=True)
            last.then_inc(s_prow, 1)

            def turn_over(t, j, r):
                pe.wait_ge(s_xn, t + 1)
                if not isinstance(t, int) or t >= 2:
                    pe.wait_ge(s_full, t - 1)
                for k in range(DC):
                    last = pe.transpose(pT[:, j % 2, k * P:(k + 1) * P], xn[:, j % 2, k * P:(k + 1) * P], ident[:])
                last.then_inc(s_tr, 1)
            skeleton(pe, ((1, turn_over),))


class Job:

    def __init__(self, first, width, count, transposed, dest, twice=False, meta=None):
        self.first, self.width, self.count, self.transposed = first, width, count, transposed
        self.dest, self.twice, self.meta = dest, twice, meta
        self.full = S // 512 if transposed else NT
        self.products = self.full + (meta is not None)


RING = 4


class Place:

    def __init__(self, i, per_tile, per_prod, tile, prod, before):
        self.i, self.pt, self.pp, self.t0, self.p0 = i, per_tile, per_prod, tile, prod
        self.before = before

    def tile(self):
        return self.i * self.pt + self.t0

    def buf(self):
        return self.t0 % 2

    def last_user(self):
        return -self.before - 1

    def slot(self, q):
        return (self.p0 + q) % RING

    def round(self, q):
        return self.i * (self.pp // RING) + (self.p0 + q) // RING


def stage_project(nc, used, tag, hT, w, jobs):
    WMAX = max(j.width * (2 if j.twice else 1) for j in jobs)
    hT_hi, hT_lo = hT
    PASSES = ((0, 0), (0, 1), (1, 0))
    wv = w[0].rearrange("(k p) n -> p k n", p=P)
    with ExitStack() as own:
        m = Memory(nc, own, used)
        w_raw = m.sb(tag + "w_raw", [P, DC, WMAX])
        w_hi = [m.sb(f"{tag}w_hi{i}", [P, DC, WMAX], F32R) for i in range(2)]
        w_lo = [m.sb(f"{tag}w_lo{i}", [P, DC, WMAX], F32R) for i in range(2)]
        stage = m.sb(tag + "stage", [P, RING, 512])
        bank = m.ps(tag + "bank", [P, RING, 512])
        s_raw = m.sem(tag + "weights_loaded")
        s_hi = m.sem(tag + "weights_high")
        s_tick = m.sem(tag + "tick")
        s_split = m.sem(tag + "weights_split")
        s_prod = [m.sem(f"{tag}product_done{i}") for i in range(RING)]
        s_evac = [m.sem(f"{tag}product_staged{i}") for i in range(RING)]
        s_out = [m.sem(f"{tag}product_stored{i}") for i in range(RING)]

        def sweep(eng, body):
            tile = prod = before = 0
            for job in jobs:
                pairs, done, per = job.count // 2, 0, 2 * job.products
                if pairs >= 2 and per % RING == 0:
                    if tile == 0:
                        done = 2
                        for n in range(2):
                            body(job, n, Place(0, 2, RING, n, n * job.products, before))
                            before = job.products
                        tile, prod, pairs = 2, per, pairs - 1
                    assert tile == 0 or before >= job.products
                    with eng.Fori(0, pairs) as i:
                        for j in range(2):
                            body(job, i * 2 + (j + done), Place(i, 2, per, tile + j, prod + j * job.products,
                                                                job.products))
                    done += 2 * pairs
                    tile += 2 * pairs
                    prod += pairs * per
                    before = job.products
                for n in range(done, job.count):
                    body(job, n, Place(0, 2, RING, tile, prod, before))
                    tile += 1
                    prod += job.products
                    before = job.products
            return prod

        def extent(job, q):
            wide = job.width * (2 if job.twice else 1)
            if q == job.full:
                at = slice(S, S + NMETA)
                return (wide, NMETA, at) if job.transposed else (NMETA, wide, at)
            if job.transposed:
                return wide, 512, slice(q * 512, (q + 1) * 512)
            return P, wide, slice(q * P, (q + 1) * P)

        block = own.enter_context(nc.Block())

        @block.sync
        def _(sp):
            def load(job, n, pl):
                sp.wait_ge(s_split, pl.tile())
                sp.dma_start(w_raw[:, :, 0:job.width], wv[:, :, ds(n * job.width + job.first, job.width)]
                             ).then_inc(s_raw, 16)
            sweep(sp, load)

        @block.gpsimd
        def _(gp):
            def split(job, n, pl):
                wd, b = job.width, pl.buf()
                gp.wait_ge(s_raw, pl.tile() * 16 + 16)
                if pl.t0 >= 2:
                    gp.wait_ge(s_prod[pl.slot(pl.last_user())], pl.round(pl.last_user()) + 1)
                gp.sem_inc(s_tick, 1)
                halves = range(2 if job.twice else 1)
                for z in halves:
                    last = gp.tensor_copy(w_hi[b][:, :, z * wd:(z + 1) * wd], w_raw[:, :, 0:wd])
                last.then_inc(s_hi, 1)
                gp.wait_ge(s_hi, pl.tile() + 1)
                for z in halves:
                    last = gp.tensor_tensor(w_lo[b][:, :, z * wd:(z + 1) * wd], w_raw[:, :, 0:wd],
                                            w_hi[b][:, :, z * wd:(z + 1) * wd].bitcast(F32), ALU.subtract)
                last.then_inc(s_split, 1)
            sweep(gp, split)

        @block.tensor
        def _(pe):
            def multiply(job, n, pl):
                b = pl.buf()
                pe.wait_ge(s_split, pl.tile() + 1)
                for q in range(job.products):
                    k = pl.slot(q)
                    pe.wait_ge(s_evac[k], pl.round(q))
                    rows, width, at = extent(job, q)
                    for c in range(DC):
                        for a, (ph, pw) in enumerate(PASSES):
                            hs = (hT_hi, hT_lo)[ph][:, c, at]
                            ws = (w_hi, w_lo)[pw][b][:, c, 0:job.width * (2 if job.twice else 1)]
                            lhsT, rhs = (ws, hs) if job.transposed else (hs, ws)
                            last = pe.matmul(bank[0:rows, k, 0:width], lhsT=lhsT, rhs=rhs,
                                             start=(c == 0 and a == 0), stop=(c == DC - 1 and a == 2))
                    last.then_inc(s_prod[k], 1)
            sweep(pe, multiply)

        @block.scalar
        def _(act):
            def body(job, n, pl):
                for q in range(job.products):
                    k = pl.slot(q)
                    rows, width, at = extent(job, q)
                    if k % 2 == 0:
                        act.wait_ge(s_prod[k], pl.round(q) + 1)
                        act.wait_ge(s_out[k], pl.round(q) * 16)
                        act.activation(stage[0:rows, k, 0:width], bank[0:rows, k, 0:width], ACT.Copy
                                       ).then_inc(s_evac[k], 1)
                    act.wait_ge(s_evac[k], pl.round(q) + 1)
                    if q == job.full:
                        dest = (job.meta[ds(n * job.width, rows), :] if job.transposed
                                else job.meta[:, ds(n * job.width, width)])
                    elif job.transposed:
                        dest = job.dest[ds(n * rows, rows), at]
                    else:
                        dest = job.dest[at, ds(n * job.width, width)]
                    act.dma_start(dest, stage[0:rows, k, 0:width]).then_inc(s_out[k], 16)
            total = sweep(act, body)
            for k in range(RING):
                act.wait_ge(s_out[k], 16 * ((total - k + RING - 1) // RING))

        @block.vector
        def _(v):
            def body(job, n, pl):
                for q in range(job.products):
                    k = pl.slot(q)
                    if k % 2 == 1:
                        rows, width, at = extent(job, q)
                        v.wait_ge(s_prod[k], pl.round(q) + 1)
                        v.wait_ge(s_out[k], pl.round(q) * 16)
                        v.tensor_copy(stage[0:rows, k, 0:width], bank[0:rows, k, 0:width]).then_inc(s_evac[k], 1)
            sweep(v, body)


R1_FIRST, R1_GROUPS, R1_WIDTH = 1020, 6, 386
R1_COLS = R1_GROUPS * R1_WIDTH
VA, FA, ZA, QB, KB, VB, ZB = (v - R1_FIRST for v in (1024, 1536, 1544, 2056, 2568, 2696, 2824))
HD = 64
H = 8


def make_masks(gp, own_, ident, mask_diag=None, mask_prev=None):
    own_.up(gp.memset(ident, 0.0))
    own_.settle()
    own_.up(gp.affine_select(out=ident, in_=ident, compare_op=ALU.not_equal, fill=1.0, base=0,
                             pattern=[[-1, P]], channel_multiplier=1))
    for mk, op_base in ((mask_diag, 0), (mask_prev, 1)):
        if mk is None:
            continue
        own_.up(gp.memset(mk, 0.0))
        own_.settle()
        if op_base == 0:
            own_.up(gp.affine_select(out=mk, in_=mk, compare_op=ALU.is_ge, fill=NEG, base=0,
                                     pattern=[[-1, P]], channel_multiplier=1))
        else:
            own_.up(gp.affine_select(out=mk, in_=mk, compare_op=ALU.is_gt, fill=NEG, base=0,
                                     pattern=[[1, P]], channel_multiplier=-1))
    own_.settle()


def stage_window(nc, used, R1, positions, inv_freq, b_fgate, sinks, cum2, OB):
    TWO_PI = 2.0 * np.pi
    C1 = float(np.float32(6.28125))
    C2 = float(np.float32(round((TWO_PI - C1) * 2**20) / 2**20))
    C3 = float(np.float32(TWO_PI - C1 - C2))
    ROUND = 12582912.0
    with ExitStack() as own:
        m = Memory(nc, own, used)
        ident = m.sb("identW", [P, P])
        identb = m.sb("identWb", [P, P], BF16)
        maskf = m.sb("maskWf", [P, 2, P])
        mask4 = m.sb("maskW4", [P, 2, 2, P], BF16)
        mask0 = m.sb("maskW0", [P, 2, 2, P], BF16)
        pos_i = m.sb("pos_i", [P, NT], I32)
        pos = m.sb("pos", [P, NT])
        freq = m.sb("freq", [P, 32])
        ang, turn, red = (m.sb(n, [P, NT, 32]) for n in ("ang", "turn", "red"))
        sin, cos = m.sb("sinW", [P, NT, 32]), m.sb("cosW", [P, NT, 32])
        f_row = m.sb("f_row", [P, NT, H])
        bf = m.sb("bf", [P, H])
        fT, fa, fe, fl, ones8 = (m.sb(n, [H, S]) for n in ("fT", "f_abs", "f_exp", "f_log", "ones8"))
        cum_hi, cum_lo = (m.sb(n, [H, S], F32R) for n in ("cum_hi", "cum_lo"))
        snk = m.sb("snk", [P, H])
        rows = m.sb("rowsW", [P, NT, 10, 2, 32])
        vt = m.sb("vtW", [P, NT, 2 * HD])
        rot = m.sb("rotW", [P, 2, 5, 2, 2, 32])
        t1, t2 = m.sb("ropet1", [P, 10, 32]), m.sb("ropet2", [P, 10, 32])
        T = m.sb("TW", [P, 2, 5, P])
        mx, mm_, nm, sm, es, rs, den, rden = (m.sb(n, [P, 2, 4]) for n in
                                              ("mxW", "mW", "nmW", "smW", "esW", "rsW", "denW", "rdenW"))
        pr = m.sb("prW", [P, 2, 4, 2, P])
        PT = m.sb("PTW", [P, 2, 4, P])
        ob = m.sb("obW", [P, 2, 2, 4 * HD])
        pS = m.ps("pSW", [P, 2, 4, 2, P])
        pPT = m.ps("pPTW", [P, 2, 4, P])
        pT = m.ps("pTW", [P, 4, P])
        pO = m.ps("pOW", [P, 512])

        s_in = m.sem("w_constants_loaded")
        s_rows = m.sem("w_rows_loaded")
        s_const = m.sem("w_constants_made")
        s_gp = m.sem("w_pool_own")
        s_tick = m.sem("w_tick")
        s_dve = m.sem("w_dve_own")
        s_act = m.sem("w_act_own")
        s_angle = m.sem("w_angles_reduced")
        s_trig = m.sem("w_sin_cos")
        s_ft = m.sem("w_f_transposed")
        s_fcopy = m.sem("w_f_copied")
        s_fabs = m.sem("w_f_abs")
        s_flog = m.sem("w_f_log")
        s_cum = m.sem("w_cum_made")
        s_rot = m.sem("w_rotated")
        s_tr = m.sem("w_transposed")
        s_T = m.sem("w_transposes_copied")
        s_sc = m.sem("w_scores")
        s_nm = m.sem("w_negated_max")
        s_ex = m.sem("w_exponentials")
        s_pt = [m.sem(f"w_probs_transposed{i}") for i in range(2)]
        s_ptc = [m.sem(f"w_probs_copied{i}") for i in range(2)]
        s_pv = m.sem("w_values_summed")
        s_ob = m.sem("w_output_rows")
        s_st = [m.sem(f"w_output_stored{i}") for i in range(2)]
        s_cst = m.sem("w_cum_stored")

        def tiles(eng, body):
            for n in range(2):
                body(n, n, n == 0)
            with eng.Fori(1, NT // 2) as i:
                for par in range(2):
                    body(i * 2 + par, par, False)

        f_ready = []

        block = own.enter_context(nc.Block())

        @block.sync
        def _(sp):
            with nc.allow_non_contiguous_dma(reason="positions and forget gates, a few KB"):
                sp.dma_start(pos_i[:], positions.rearrange("a (t p) -> p (a t)", p=P)).then_inc(s_in, 16)
                sp.dma_start(f_row[:], R1[:, FA:FA + H].rearrange("(t p) h -> p t h", p=P)).then_inc(s_in, 16)
            sp.dma_start(freq[:], inv_freq.to_broadcast([P, 32])).then_inc(s_in, 16)
            sp.dma_start(bf[:], b_fgate.to_broadcast([P, H])).then_inc(s_in, 16)
            sp.dma_start(snk[:], sinks.to_broadcast([P, H])).then_inc(s_in, 16)

            for i in range(4):
                sp.dma_start(rows[:, 4 * i:4 * i + 4].rearrange("p t a b c -> p t (a b c)"),
                             R1[i * 4 * P:(i + 1) * 4 * P, QB:QB + 640].rearrange("(t p) c -> p t c", p=P)
                             ).then_inc(s_rows, 16)
            sp.dma_start(vt[:], R1[:, VB:VB + 2 * HD].rearrange("(t p) c -> p t c", p=P)).then_inc(s_rows, 16)

            def store(n, par, first):
                sp.wait_ge(s_ob, n * 2 + 2)
                sp.dma_start(OB[ds(n * P, P), :], ob[:, par].rearrange("p g d -> p (g d)")).then_inc(s_st[par], 16)
            tiles(sp, store)
            for par in range(2):
                sp.wait_ge(s_st[par], 8 * NT)
            sp.wait_ge(s_cst, 32)

        @block.gpsimd
        def _(gp):
            own_ = Tally(gp, s_gp)
            make_masks(gp, own_, ident[:], maskf[:, 1, :], maskf[:, 0, :])
            gp.tensor_copy(identb[:], ident[:])
            for z in range(2):
                gp.tensor_copy(mask4[:, z], maskf[:])
                gp.tensor_copy(mask0[:, z, 1, :], maskf[:, 1, :])
                last = gp.memset(mask0[:, z, 0, :], NEG)
            own_.up(last)
            own_.up(gp.memset(T[:, 1, 4, :], 0.0))
            gp.memset(ones8[:], 1.0).then_inc(s_const, 1)

            gp.wait_ge(s_trig, 2)
            gp.wait_ge(s_rows, 80)

            def rope(n, par, first):
                if not isinstance(n, int):
                    gp.wait_ge(s_tr, n * 2 - 2)
                c_ = cos[:, ds(n, 1), :].to_broadcast([P, 10, 32])
                s_ = sin[:, ds(n, 1), :].to_broadcast([P, 10, 32])
                x1, x2 = (rows[:, ds(n, 1), :, z, :].rearrange("p a b c -> p (a b) c") for z in range(2))
                def out(z):
                    return (rot[:, par, 0:4, :, z, :].rearrange("p a b c -> p b a c"), rot[:, par, 4, :, z, :])
                for z, (a, b, op) in enumerate(((x1, x2, ALU.subtract), (x2, x1, ALU.add))):
                    gp.sem_inc(s_tick, 1)
                    own_.up(gp.tensor_tensor(t1[:], a, c_, ALU.mult))
                    own_.up(gp.tensor_tensor(t2[:], b, s_, ALU.mult))
                    own_.settle()
                    q_, k_ = out(z)
                    own_.up(gp.tensor_tensor(q_, t1[:, 0:8, :].rearrange("p (b a) c -> p b a c", b=2),
                                             t2[:, 0:8, :].rearrange("p (b a) c -> p b a c", b=2), op))
                    last = gp.tensor_tensor(k_, t1[:, 8:10, :], t2[:, 8:10, :], op)
                    if z == 0:
                        own_.up(last)
                        own_.settle()
                    else:
                        own_.settle()
                        last.then_inc(s_rot, 1)
                        gp.wait_ge(s_rot, n + 1)
            for n in range(2):
                rope(n, n, n == 0)
            with gp.Fori(1, NT // 2) as i:
                own_.enter(i - 1, 14)
                for par in range(2):
                    rope(i * 2 + par, par, False)
                own_.leave(NT // 2 - 1)

        @block.scalar
        def _(act):
            act.wait_ge(s_angle, 1)
            act.activation(sin[:], red[:], ACT.Sin).then_inc(s_trig, 1)
            act.wait_ge(s_angle, 2)
            act.activation(cos[:], ang[:], ACT.Sin).then_inc(s_trig, 1)
            act.wait_ge(s_fcopy, 1)
            act.activation(fa[:], fT[:], ACT.Abs).then_inc(s_fabs, 1)
            act.wait_ge(s_fabs, 1)
            act.activation(fe[:], fa[:], ACT.Exp, scale=-1.0).then_inc(s_act, 1)
            act.wait_ge(s_act, 1)
            act.activation(fl[:], fe[:], ACT.Ln, bias=1.0).then_inc(s_flog, 1)
            act.wait_ge(s_cum, 1)
            parts = cum2.rearrange("(h z) s -> h z s", z=2)
            act.dma_start(parts[:, 0], cum_hi[:].bitcast(F32)).then_inc(s_cst, 16)
            act.dma_start(parts[:, 1], cum_lo[:].bitcast(F32)).then_inc(s_cst, 16)

            def exps(n, g, par):
                s = n * 2 + g
                act.wait_ge(s_nm, s + 1)
                if not isinstance(n, int) or n >= 1:
                    act.wait_ge(s_pt[0], s - 1)
                    act.wait_ge(s_pt[1], s - 1)
                for j in range(4):
                    act.activation(pr[:, g, j], pS[:, g, j], ACT.Exp, bias=nm[:, g, j:j + 1], scale=0.125,
                                   accum_out=rs[:, g, j:j + 1])
                act.activation(es[:, g, :], sm[:, g, :], ACT.Exp).then_inc(s_ex, 1)

            def copy_probs(s):
                act.wait_ge(s_pt[0], s + 1)
                act.wait_ge(s_pv, s)
                act.activation(PT[:, 0], pPT[:, 0], ACT.Copy).then_inc(s_ptc[0], 1)

            def body(n, par, first):
                for g in range(2):
                    exps(n, g, par)
                    if not (first and g == 0):
                        copy_probs(n * 2 + g - 1)
            tiles(act, body)
            copy_probs(2 * NT - 1)

        @block.vector
        def _(v):
            own_ = Tally(v, s_dve)
            v.wait_ge(s_in, 80)
            own_.up(v.tensor_copy(pos[:], pos_i[:]))
            own_.settle()
            own_.up(v.tensor_tensor(ang[:], pos[:].unsqueeze(2).to_broadcast([P, NT, 32]),
                                    freq[:].unsqueeze(1).to_broadcast([P, NT, 32]), ALU.mult))
            own_.settle()
            for z in range(2):
                own_.up(v.tensor_scalar(turn[:], ang[:], 1.0 / TWO_PI, 0.25 * z, ALU.mult, ALU.add))
                own_.settle()
                own_.up(v.tensor_scalar(turn[:], turn[:], ROUND, -ROUND, ALU.add, ALU.add))
                own_.settle()
                dst = red if z == 0 else ang
                own_.up(v.scalar_tensor_tensor(dst[:], turn[:], -C1, ang[:], ALU.mult, ALU.add))
                own_.settle()
                own_.up(v.scalar_tensor_tensor(dst[:], turn[:], -C2, dst[:], ALU.mult, ALU.add))
                own_.settle()
                own_.up(v.scalar_tensor_tensor(dst[:], turn[:], -C3, dst[:], ALU.mult, ALU.add))
                own_.settle()
                if z == 1:
                    own_.up(v.tensor_scalar(dst[:], dst[:], np.pi / 2, None, ALU.add))
                    own_.settle()
                v.tensor_scalar(dst[:], dst[:], 3.14159, -3.14159, ALU.min, ALU.max).then_inc(s_angle, 1)
            own_.up(v.tensor_tensor(f_row[:], f_row[:], bf[:].unsqueeze(1).to_broadcast([P, NT, H]), ALU.add))
            own_.settle()
            f_ready.append(own_.at)
            v.wait_ge(s_ft, 1)
            v.tensor_copy(fT[:].rearrange("h (a b) -> h a b", b=1024),
                          pS[0:H].rearrange("p g j z k -> p (g j z k)").rearrange("p (a b) -> p a b", b=1024)
                          ).then_inc(s_fcopy, 1)
            v.wait_ge(s_flog, 1)
            own_.up(v.scalar_tensor_tensor(fe[:], fT[:], 0.0, fl[:], ALU.min, ALU.subtract))
            v.wait_ge(s_const, 1)
            own_.settle()
            own_.up(v.tensor_tensor_scan(fl[:], ones8[:], fe[:], 0.0, ALU.mult, ALU.add))
            own_.settle()
            own_.up(v.tensor_scalar(fT[:], fl[:], -8.0, None, ALU.mult))
            own_.settle()
            own_.up(v.tensor_copy(cum_hi[:], fT[:]))
            own_.settle()
            v.tensor_tensor(cum_lo[:], fT[:], cum_hi[:].bitcast(F32), ALU.subtract).then_inc(s_cum, 1)

            def copy_T(n, par):
                v.wait_ge(s_tr, n * 2 + 1)
                v.tensor_copy(T[:, par, 0:4, :], pT[:]).then_inc(s_T, 1)
                v.wait_ge(s_tr, n * 2 + 2)
                v.tensor_copy(T[:, par, 4, :], pT[:, 0, :]).then_inc(s_T, 1)

            def maxima(n, g):
                s = n * 2 + g
                v.wait_ge(s_sc, s + 1)
                own_.up(v.tensor_reduce(mx[:, g, :], pS[:, g].rearrange("p j z k -> p j (z k)"), AX.X, ALU.max))
                own_.settle()
                own_.up(v.scalar_tensor_tensor(mm_[:, g, :], mx[:, g, :], 0.125, snk[:, 4 * g:4 * g + 4],
                                               ALU.mult, ALU.max))
                own_.settle()
                if not isinstance(n, int) or n >= 1:
                    v.wait_ge(s_ex, s - 1)
                own_.up(v.tensor_scalar(nm[:, g, :], mm_[:, g, :], -1.0, None, ALU.mult))
                own_.settle()
                v.tensor_tensor(sm[:, g, :], snk[:, 4 * g:4 * g + 4], nm[:, g, :], ALU.add).then_inc(s_nm, 1)

            def finish(n, g, par):
                s = n * 2 + g
                v.wait_ge(s_pt[1], s + 1)
                v.wait_ge(s_pv, s)
                v.tensor_copy(PT[:, 1], pPT[:, 1]).then_inc(s_ptc[1], 1)
                own_.up(v.tensor_tensor(den[:, g, :], rs[:, g, :], es[:, g, :], ALU.add))
                own_.settle()
                own_.up(v.reciprocal(rden[:, g, :], den[:, g, :]))
                own_.settle()
                v.wait_ge(s_pv, s + 1)
                if g == 0:
                    v.wait_ge(s_st[par], out_round(n))
                v.tensor_tensor(ob[:, par, g, :].rearrange("p (j d) -> p j d", d=HD),
                                pO[:, 0:4 * HD].rearrange("p (j d) -> p j d", d=HD),
                                rden[:, g, :].unsqueeze(2).to_broadcast([P, 4, HD]), ALU.mult).then_inc(s_ob, 1)

            def out_round(n):
                return 16 * (n // 2) if isinstance(n, int) else stores[0] * 16

            stores = [0]
            copy_T(0, 0)
            maxima(0, 0)
            maxima(0, 1)
            finish(0, 0, 0)
            copy_T(1, 1)
            maxima(1, 0)
            finish(0, 1, 0)
            maxima(1, 1)
            finish(1, 0, 1)
            with v.Fori(1, NT // 2) as i:
                own_.enter(i - 1, 20)
                for par in range(2):
                    n = i * 2 + par
                    copy_T(n, par)
                    maxima(n, 0)
                    stores[0] = i + (par - 1)
                    finish(n - 1, 1, 1 - par)
                    maxima(n, 1)
                    stores[0] = i
                    finish(n, 0, par)
                own_.leave(NT // 2 - 1)
            finish(NT - 1, 1, 1)

        @block.tensor
        def _(pe):
            pe.wait_ge(s_gp, 7)
            pe.wait_ge(s_const, 1)
            pe.wait_ge(s_dve, f_ready[0])
            pe.wait_ge(s_rows, 80)
            for t in range(NT):
                last = pe.transpose(pS[0:H].rearrange("p g j z k -> p (g j z k)")[:, t * P:(t + 1) * P],
                                    f_row[:, t, :], ident[:])
            last.then_inc(s_ft, 1)
            pe.wait_ge(s_fcopy, 1)

            def turn_over(n, par):
                pe.wait_ge(s_rot, n + 1)
                if not isinstance(n, int) or n >= 1:
                    pe.wait_ge(s_T, n * 2)
                for j in range(4):
                    last = pe.transpose(pT[:, j, :], rot[:, par, j].rearrange("p b z c -> p (b z c)"), ident[:])
                last.then_inc(s_tr, 1)
                pe.wait_ge(s_T, n * 2 + 1)
                pe.transpose(pT[:, 0, :], rot[:, par, 4].rearrange("p b z c -> p (b z c)"), ident[:]).then_inc(s_tr, 1)

            def scores(n, g, par, first):
                s = n * 2 + g
                if g == 0:
                    pe.wait_ge(s_T, n * 2 + 2)
                if not isinstance(n, int) or n >= 1:
                    pe.wait_ge(s_ex, s - 1)
                half = slice(HD * g, HD * g + HD)
                for b in range(2):
                    pe.matmul(pS[:, g, 2 * b:2 * b + 2], lhsT=identb[:], rhs=(mask0 if first else mask4)[:],
                              start=True, stop=False, skip_group_check=True)
                for j in range(4):
                    for z, kp in ((0, 1 - par), (1, par)):
                        if first and z == 0:
                            continue
                        last = pe.matmul(pS[:, g, j, z, :], lhsT=T[half, par, j, :], rhs=T[half, kp, 4, :],
                                         start=False, stop=True, skip_group_check=True)
                last.then_inc(s_sc, 1)

            def values(n, g, par, first):
                s = n * 2 + g
                pe.wait_ge(s_ex, s + 1)
                for u in range(2):
                    if not (first and g == 0):
                        pe.wait_ge(s_ptc[u], s)
                    for j in range(2):
                        for z in range(2):
                            last = pe.transpose(pPT[:, u, 2 * j + z, :], pr[:, g, 2 * u + j, z, :], ident[:])
                    last.then_inc(s_pt[u], 1)
                if not (first and g == 0):
                    pe.wait_ge(s_ob, s)
                for u in range(2):
                    pe.wait_ge(s_ptc[u], s + 1)
                    for j in range(2):
                        for z in ((1,) if first else (0, 1)):
                            last = pe.matmul(pO[:, (2 * u + j) * HD:(2 * u + j + 1) * HD],
                                             lhsT=PT[:, u, 2 * j + z, :],
                                             rhs=vt[:, ds(n - 1 + z, 1), g * HD:(g + 1) * HD],
                                             start=(z == 1 and first) or z == 0, stop=(z == 1))
                last.then_inc(s_pv, 1)

            turn_over(0, 0)
            scores(0, 0, 0, True)
            scores(0, 1, 0, True)
            values(0, 0, 0, True)
            turn_over(1, 1)
            scores(1, 0, 1, False)
            values(0, 1, 0, True)
            scores(1, 1, 1, False)
            values(1, 0, 1, False)
            with pe.Fori(1, NT // 2) as i:
                for par in range(2):
                    n = i * 2 + par
                    turn_over(n, par)
                    scores(n, 0, par, False)
                    values(n - 1, 1, 1 - par, False)
                    scores(n, 1, par, False)
                    values(n, 0, par, False)
            values(NT - 1, 1, 1, False)


def stage_forget(nc, used, QK, cum2, R1, OA):
    CH = 512
    chunks = [-(-(i + 1) * P // CH) for i in range(NT)]
    before = [sum(chunks[:i]) for i in range(NT)]
    PER = sum(chunks)
    KR, TR = 4, 2
    with ExitStack() as own:
        m = Memory(nc, own, used)
        ident = m.sb("identF", [P, P])
        identb = m.sb("identFb", [P, P], BF16)
        maskf = m.sb("maskFf", [P, P])
        mask = m.sb("maskF", [P, P], BF16)
        rawq, rawk = m.sb("rawq", [P, S]), m.sb("rawk", [P, S])
        kh = m.sb("khF", [P, S], F32R)
        qh, ql, ks, k2 = ([m.sb(f"{n}{b}", [P, S], F32R) for b in range(2)] for n in ("qh", "ql", "ks", "k2"))
        vv = m.sb("vvF", [P, 2, NT, HD + 1])
        sc = m.sb("scF", [P, 4, S])
        PT = m.sb("PTF", [P, TR, 4, P])
        mxc = m.sb("mxcF", [P, 2, 4])
        mx, nm = m.sb("mxF", [P, 2]), m.sb("nmF", [P, 4])
        rd = m.sb("rdF", [P, 2])
        oh = m.sb("ohF", [P, 2, NT, HD])
        pS = m.ps("pSF", [P, KR, CH])
        pPT = m.ps("pPTF", [P, TR, 4, P])
        pO = m.ps("pOF", [P, 2, 512])

        s_raw = m.sem("f_heads_loaded")
        s_cv = [m.sem(f"f_cum_values_loaded{b}") for b in range(2)]
        s_const = m.sem("f_constants_made")
        s_split = m.sem("f_heads_split")
        s_sc = [m.sem(f"f_scores{k}") for k in range(KR)]
        s_cp = [m.sem(f"f_scores_copied{k}") for k in range(KR)]
        s_nm = m.sem("f_negated_max")
        s_ex = m.sem("f_probabilities")
        s_pt = [m.sem(f"f_probs_transposed{k}") for k in range(TR)]
        s_ptc = [m.sem(f"f_probs_copied{k}") for k in range(TR)]
        s_pv = [m.sem(f"f_values_summed{k}") for k in range(2)]
        s_o = [m.sem(f"f_output_scaled{k}") for k in range(2)]
        s_st = m.sem("f_output_stored")
        s_dve = m.sem("f_dve_own")
        s_gp = m.sem("f_pool_own")
        s_tick = m.sem("f_tick")

        block = own.enter_context(nc.Block())

        @block.sync
        def _(sp):
            def load(hd, b, reused):
                sp.wait_ge(s_split, hd * 6)
                for half in range(2):
                    sp.dma_start(rawq[half * HD:(half + 1) * HD, :], QK[ds(hd * HD, HD), :]).then_inc(s_raw, 16)
                    sp.dma_start(rawk[half * HD:(half + 1) * HD, :], QK[ds(hd * HD + H * HD, HD), :]
                                 ).then_inc(s_raw, 16)
                if reused:
                    sp.wait_ge(s_pv[1], hd * 8 - 8)
                sp.dma_start(k2[b][HD:HD + 2, :].bitcast(F32), cum2[ds(hd * 2, 2), :]).then_inc(s_cv[b], 16)
                sp.dma_start(vv[:, b, :, 0:HD],
                             R1[:, ds(hd * HD + VA, HD)].rearrange("(t p) d -> p t d", p=P)).then_inc(s_cv[b], 16)

            def store(hd, b):
                for k in range(2):
                    sp.wait_ge(s_o[k], hd * 8 + 8)
                sp.dma_start(OA[:, ds(hd * HD, HD)].rearrange("(t p) d -> p t d", p=P), oh[:, b]).then_inc(s_st, 16)

            for b in range(2):
                load(b, b, False)
            with sp.Fori(1, H // 2) as i:
                for b in range(2):
                    load(i * 2 + b, b, True)
                    store(i * 2 + b - 2, b)
            for b in range(2):
                store(H - 2 + b, b)
            sp.wait_ge(s_st, 16 * H)

        @block.gpsimd
        def _(gp):
            own_ = Tally(gp, s_gp)
            make_masks(gp, own_, ident[:], maskf[:])
            gp.tensor_copy(identb[:], ident[:]).then_inc(s_const, 1)
            gp.tensor_copy(mask[:], maskf[:]).then_inc(s_const, 1)
            gp.memset(vv[:, :, :, HD:HD + 1], 1.0).then_inc(s_const, 1)
            for b in range(2):
                gp.wait_ge(s_const, 3 + b)
                gp.memset(ql[b][HD:HD + 2, :].bitcast(F32), 1.0).then_inc(s_const, 1)
            gp.wait_ge(s_const, 5)

            def split(hd, b, reused):
                gp.wait_ge(s_raw, hd * 64 + 64)
                if reused:
                    gp.wait_ge(s_sc[KR - 1], hd * 10 - 10)
                gp.sem_inc(s_tick, 1)
                lower, upper = slice(0, HD), slice(HD, P)
                steps = ((gp.tensor_copy, qh[b][:], rawq[:]),
                         (gp.tensor_copy, ks[b][lower], rawk[lower]),
                         (gp.tensor_copy, k2[b][lower], rawk[lower]),
                         (gp.tensor_tensor, ql[b][lower], rawq[lower], qh[b][lower].bitcast(F32), ALU.subtract),
                         (gp.tensor_copy, kh[upper], rawk[upper]),
                         (gp.tensor_tensor, ks[b][upper], rawk[upper], kh[upper].bitcast(F32), ALU.subtract))
                for z, (op, *operands) in enumerate(steps):
                    op(*operands).then_inc(s_split, 1)
                    gp.wait_ge(s_split, hd * 6 + (z + 1))
                    gp.sem_inc(s_tick, 1)
            for b in range(2):
                split(b, b, False)
            with gp.Fori(1, H // 2) as i:
                for b in range(2):
                    split(i * 2 + b, b, True)

        STEPS = 2 * NT
        LAG = 2

        def chunk(s, c):
            return (s // NT) * PER + before[s % NT] + c

        def nth(turn, g, ring, per=2 * PER):
            return turn * (per // ring) + g // ring

        def width(i, c):
            return min(CH, (i + 1) * P - c * CH)

        def copies(act, turn, s):
            i = s % NT
            for c in range(chunks[i]):
                g = chunk(s, c)
                k, w = g % TR, width(i, c)
                act.wait_ge(s_pt[k], nth(turn, g, TR) + 1)
                act.copy(PT[:, k, 0:w // P, :], pPT[:, k, 0:w // P, :]).then_inc(s_ptc[k], 1)

        @block.tensor
        def _(pe):
            def scores(turn, s):
                b, i = divmod(s, NT)
                if i == 0:
                    hd = turn * 2 + b
                    pe.wait_ge(s_split, hd * 6 + 6)
                    pe.wait_ge(s_cv[b], turn * 32 + 32)
                at = slice(i * P, (i + 1) * P)
                for c in range(chunks[i]):
                    g = chunk(s, c)
                    k = g % KR
                    w = width(i, c)
                    keys = slice(c * CH, c * CH + w)
                    diag = c == chunks[i] - 1
                    pe.wait_ge(s_cp[k], nth(turn, g, KR))
                    pe.matmul(pS[:, k, 0:w], lhsT=qh[b][:, at], rhs=ks[b][:, keys], start=True, stop=False)
                    last = pe.matmul(pS[:, k, 0:w], lhsT=ql[b][0:HD + 2, at], rhs=k2[b][0:HD + 2, keys],
                                     start=False, stop=True)
                    if diag:
                        last = pe.matmul(pS[:, k, w - P:w], lhsT=identb[:], rhs=mask[:], start=False, stop=True,
                                         skip_group_check=True)
                    last.then_inc(s_sc[k], 1)

            def turn_over(turn, s, c):
                i, g = s % NT, chunk(s, c)
                k = g % TR
                pe.wait_ge(s_ptc[k], nth(turn, g, TR))
                for t in range(width(i, c) // P):
                    last = pe.transpose(pPT[:, k, t, :], sc[:, s % 4, c * CH + t * P:c * CH + (t + 1) * P], ident[:])
                last.then_inc(s_pt[k], 1)

            def add(turn, s, c):
                b, i = divmod(s, NT)
                g = chunk(s, c)
                k = g % TR
                pe.wait_ge(s_ptc[k], nth(turn, g, TR) + 1)
                for t in range(width(i, c) // P):
                    kt = c * 4 + t
                    last = pe.matmul(pO[:, s % 2, 0:HD + 1], lhsT=PT[:, k, t, :], rhs=vv[:, b, kt, :],
                                     start=(kt == 0), stop=(kt == i))
                return last
            def values(turn, s):
                n = chunks[s % NT]
                pe.wait_ge(s_ex, turn * STEPS + s + 1)
                turn_over(turn, s, 0)
                for c in range(1, n):
                    turn_over(turn, s, c)
                    if c == 1:
                        pe.wait_ge(s_o[s % 2], nth(turn, s, 2, STEPS))
                    add(turn, s, c - 1)

            def last_values(turn, s):
                n = chunks[s % NT]
                if n == 1:
                    pe.wait_ge(s_o[s % 2], nth(turn, s, 2, STEPS))
                add(turn, s, n - 1).then_inc(s_pv[s % 2], 1)

            pe.wait_ge(s_const, 5)
            with pe.Fori(0, H // 2) as turn:
                for s in range(STEPS + LAG):
                    if s >= LAG:
                        values(turn, s - LAG)
                    if s < STEPS:
                        scores(turn, s)
                    if s >= LAG:
                        last_values(turn, s - LAG)

        @block.vector
        def _(v):
            own_ = Tally(v, s_dve)

            def maxima(turn, s):
                b, i = divmod(s, NT)
                if s >= 4:
                    v.wait_ge(s_pv[s % 2], nth(turn, s - 4, 2, STEPS) + 1)
                n = chunks[i]
                for c in range(n):
                    g = chunk(s, c)
                    k, w = g % KR, width(i, c)
                    v.wait_ge(s_sc[k], nth(turn, g, KR) + 1)
                    v.tensor_scalar(sc[:, s % 4, c * CH:c * CH + w], pS[:, k, 0:w], 1.0, None, ALU.mult, ALU.max,
                                    accum_out=mxc[:, s % 2, c:c + 1]).then_inc(s_cp[k], 1)
                for k in range(min(n, KR)):
                    g = chunk(s, n - 1 - k)
                    v.wait_ge(s_cp[g % KR], nth(turn, g, KR) + 1)
                own_.up(v.tensor_reduce(mx[:, s % 2:s % 2 + 1], mxc[:, s % 2, 0:n], AX.X, ALU.max))
                own_.settle()
                v.tensor_scalar(nm[:, s % 4:s % 4 + 1], mx[:, s % 2:s % 2 + 1], -0.125, None, ALU.mult
                                ).then_inc(s_nm, 1)

            def scale(turn, s):
                b, i = divmod(s, NT)
                v.wait_ge(s_pv[s % 2], nth(turn, s, 2, STEPS) + 1)
                own_.up(v.reciprocal(rd[:, s % 2:s % 2 + 1], pO[:, s % 2, HD:HD + 1]))
                if i == 0:
                    v.wait_ge(s_st, turn * 32)
                own_.settle()
                v.tensor_scalar(oh[:, b, i, :], pO[:, s % 2, 0:HD], rd[:, s % 2:s % 2 + 1], None, ALU.mult
                                ).then_inc(s_o[s % 2], 1)

            with v.Fori(0, H // 2) as turn:
                own_.enter(turn, 2 * STEPS)
                for s in range(STEPS + LAG):
                    if s < STEPS:
                        maxima(turn, s)
                    if s >= LAG:
                        scale(turn, s - LAG)
                own_.leave(H // 2)

        @block.scalar
        def _(act):
            def exps(turn, s):
                n = (s % NT + 1) * P
                act.wait_ge(s_nm, turn * STEPS + s + 1)
                act.activation(sc[:, s % 4, 0:n], sc[:, s % 4, 0:n], ACT.Exp, bias=nm[:, s % 4:s % 4 + 1], scale=0.125
                               ).then_inc(s_ex, 1)

            with act.Fori(0, H // 2) as turn:
                for s in range(STEPS + LAG):
                    if s >= LAG:
                        copies(act, turn, s - LAG)
                    if 1 <= s <= STEPS:
                        exps(turn, s - 1)


DN_ALPHA = 2.0 ** 0.25


def stage_out(nc, used, tag, parts, gates, w_out, rows_in, rows_out, gate_row=None, ln=None):
    HW = D // 2
    PASSES = ((0, 0), (0, 1), (1, 0))
    with ExitStack() as own:
        m = Memory(nc, own, used)
        n_ = lambda s: tag + s
        ident = m.sb(n_("ident"), [P, P])
        wraw = m.sb(n_("wraw"), [P, DC, D])
        w_hi, w_lo = m.sb(n_("whi"), [P, DC, D], F32R), m.sb(n_("wlo"), [P, DC, D], F32R)
        og, zg, xg = (m.sb(n_(s), [P, 2, D]) for s in ("og", "zg", "xg"))
        sig = m.sb(n_("sig"), [P, D])
        g1 = m.sb(n_("g1"), [P, 2, D])
        G_hi = [m.sb(n_(f"Ghi{i}"), [P, DC, P], F32R) for i in range(2)]
        G_lo = [m.sb(n_(f"Glo{i}"), [P, DC, P], F32R) for i in range(2)]
        junk = m.sb(n_("junk"), [P, D])
        tt = m.sb(n_("tt"), [P, 2, D])
        ssq, var, std, rstd, mu, nmu = (m.sb(n_(s), [P, 2]) for s in ("ssq", "var", "std", "rstd", "mu", "nmu"))
        if ln:
            gain, offset = m.sb(n_("gain"), [P, D]), m.sb(n_("offset"), [P, D])
        pT = m.ps(n_("pT"), [P, 2, D])
        pY = m.ps(n_("pY"), [P, 2, D])

        s_w = [m.sem(n_(f"w_loaded{i}")) for i in range(DC // 2)]
        s_wh, s_wl = m.sem(n_("w_high")), [m.sem(n_(f"w_low{i}")) for i in range(2)]
        s_c = m.sem(n_("vectors_loaded"))
        s_in = [m.sem(n_(f"parts_loaded{i}")) for i in range(2)]
        s_x = [m.sem(n_(f"rows_loaded{i}")) for i in range(2)]
        s_const = m.sem(n_("identity"))
        s_gp = m.sem(n_("pool_own"))
        s_sig = m.sem(n_("sigmoid"))
        s_gated = m.sem(n_("gated"))
        s_tr = m.sem(n_("transposed"))
        s_hi, s_lo = m.sem(n_("high")), m.sem(n_("low"))
        s_y = m.sem(n_("y"))
        s_sum = m.sem(n_("residual_sum"))
        s_ssq, s_var, s_std = m.sem(n_("ssq")), m.sem(n_("var")), m.sem(n_("root"))
        s_res = [m.sem(n_(f"result{i}")) for i in range(2)]
        s_st = [m.sem(n_(f"stored{i}")) for i in range(2)]
        s_dve = m.sem(n_("dve_own"))

        FIRST, LAST, AHEAD, BEHIND = 1, NT - 4, 3, 1

        def skeleton(eng, phases, tally=None, per=0):
            def turns(ns):
                for n in ns:
                    for off, phase in phases:
                        if 0 <= n + off < NT:
                            phase(n + off, (n + off) % 2, (n + off) // 2)
            turns(range(-AHEAD, FIRST))
            laps = (LAST - FIRST + 1) // 2
            with eng.Fori(0, laps) as i:
                if tally:
                    tally.enter(i, per)
                for par in range(2):
                    for off, phase in phases:
                        z = FIRST + par + off
                        phase(i * 2 + z, z % 2, i + z // 2)
                if tally:
                    tally.leave(laps)
            turns(range(LAST + 1, NT + BEHIND))

        block = own.enter_context(nc.Block())

        @block.sync
        def _(sp):
            if ln:
                for dst, src in ((gain, ln[0]), (offset, ln[1])):
                    sp.dma_start(dst[:], src.to_broadcast([P, D])).then_inc(s_c, 16)

            def load_parts(n, b, r):
                if not isinstance(n, int) or n >= 2:
                    sp.wait_ge(s_gated, n - 1)
                at = ds(n * P, P)
                for z in range(2):
                    sp.dma_start(og[:, b, z * HW:(z + 1) * HW], parts[z][at, :]).then_inc(s_in[b], 16)
                    sp.dma_start(zg[:, b, z * HW:(z + 1) * HW], gates[z][at, :]).then_inc(s_in[b], 16)

            def load_rows(n, b, r):
                sp.wait_ge(s_res[b], r)
                sp.dma_start(xg[:, b, :], rows_in[ds(n * P, P), :]).then_inc(s_x[b], 16)

            def store(n, b, r):
                sp.wait_ge(s_res[b], r + 1)
                sp.dma_start(rows_out[ds(n * P, P), :], tt[:, b, :]).then_inc(s_st[b], 16)
            skeleton(sp, ((3, load_parts), (-1, store), (1, load_rows)))
            for b in range(2):
                sp.wait_ge(s_st[b], 8 * NT)

        def split_low(eng, z):
            for k in range(z, DC, 2):
                eng.wait_ge(s_wh, k + 1)
                eng.tensor_tensor(w_lo[:, k, :], wraw[:, k, :], w_hi[:, k, :].bitcast(F32), ALU.subtract
                                  ).then_inc(s_wl[z], 1)

        @block.gpsimd
        def _(gp):
            own_ = Tally(gp, s_gp)
            for k in range(0, DC, 2):
                gp.dma_start(wraw[:, k:k + 2, :], w_out[0, k * P:(k + 2) * P, :].rearrange("(k p) n -> p k n", p=P)
                             ).then_inc(s_w[k // 2], 16)
            own_.up(gp.memset(ident[:], 0.0))
            own_.settle()
            gp.affine_select(out=ident[:], in_=ident[:], compare_op=ALU.not_equal, fill=1.0, base=0,
                             pattern=[[-1, P]], channel_multiplier=1).then_inc(s_const, 1)
            split_low(gp, 1)

        @block.tensor
        def _(pe):
            pe.wait_ge(s_const, 1)

            def turn_over(n, b, r):
                pe.wait_ge(s_gated, n + 1)
                for k in range(DC):
                    last = pe.transpose(pT[:, b, k * P:(k + 1) * P], g1[:, b, k * P:(k + 1) * P], ident[:])
                last.then_inc(s_tr, 1)

            def multiply(n, b, r):
                pe.wait_ge(s_lo, n + 1)
                pe.wait_ge(s_res[b], r)
                for z in range(2):
                    for k in range(DC):
                        for a, (pg, pw) in enumerate(PASSES):
                            last = pe.matmul(pY[:, b, z * HW:(z + 1) * HW], lhsT=(G_hi, G_lo)[pg][b][:, k, :],
                                             rhs=(w_hi, w_lo)[pw][:, k, z * HW:(z + 1) * HW],
                                             start=(k == 0 and a == 0), stop=(k == DC - 1 and a == 2))
                last.then_inc(s_y, 1)
            for z in range(2):
                pe.wait_ge(s_wl[z], DC // 2)
            skeleton(pe, ((1, turn_over), (0, multiply)))

        @block.scalar
        def _(act):
            for k in range(DC):
                act.wait_ge(s_w[k // 2], 16)
                act.activation(w_hi[:, k, :], wraw[:, k, :], ACT.Copy).then_inc(s_wh, 1)

            def gate(n, b, r):
                act.wait_ge(s_in[b], r * 64 + 64)
                act.wait_ge(s_gated, n)
                act.activation(sig[:], zg[:, b, :], ACT.Sigmoid).then_inc(s_sig, 1)

            def high(n, b, r):
                act.wait_ge(s_tr, n + 1)
                act.activation(G_hi[b][:].rearrange("p a b -> p (a b)"), pT[:, b, :], ACT.Copy).then_inc(s_hi, 1)

            def finish(n, b, r):
                if ln:
                    act.wait_ge(s_sum, n + 1)
                    act.activation(junk[:], tt[:, b, :], ACT.Square, bias=nmu[:, b:b + 1],
                                   accum_out=ssq[:, b:b + 1]).then_inc(s_ssq, 1)
                else:
                    act.wait_ge(s_y, n + 1)
                    act.activation(junk[:], pY[:, b, :], ACT.Square, accum_out=ssq[:, b:b + 1]).then_inc(s_ssq, 1)
                act.wait_ge(s_var, n + 1)
                act.activation(std[:, b:b + 1], var[:, b:b + 1], ACT.Sqrt).then_inc(s_std, 1)
            skeleton(act, ((1, high), (-1, finish), (2, gate)))

        @block.vector
        def _(v):
            own_ = Tally(v, s_dve)

            split_low(v, 0)

            def gate(n, b, r):
                v.wait_ge(s_in[b], r * 64 + 64)
                own_.up(v.tensor_tensor(g1[:, b, :], og[:, b, :], zg[:, b, :], ALU.mult))
                v.wait_ge(s_sig, n + 1)
                own_.settle()
                v.tensor_tensor(g1[:, b, :], g1[:, b, :], sig[:], ALU.mult).then_inc(s_gated, 1)

            def low(n, b, r):
                v.wait_ge(s_hi, n + 1)
                v.tensor_tensor(G_lo[b][:].rearrange("p a b -> p (a b)"), pT[:, b, :],
                                G_hi[b][:].bitcast(F32).rearrange("p a b -> p (a b)"), ALU.subtract).then_inc(s_lo, 1)

            def finish(n, b, r):
                v.wait_ge(s_x[b], r * 16 + 16)
                one = slice(b, b + 1)
                v.wait_ge(s_st[b], r * 16)
                if ln:
                    v.wait_ge(s_y, n + 1)
                    own_.up(v.scalar_tensor_tensor(tt[:, b, :], xg[:, b, :], DN_ALPHA, pY[:, b, :], ALU.mult, ALU.add,
                                                   accum_out=mu[:, one]))
                    own_.settle()
                    own_.up(v.tensor_scalar(mu[:, one], mu[:, one], 1.0 / D, None, ALU.mult))
                    own_.settle()
                    v.tensor_scalar(nmu[:, one], mu[:, one], -1.0, None, ALU.mult).then_inc(s_sum, 1)
                v.wait_ge(s_ssq, n + 1)
                v.tensor_scalar(var[:, one], ssq[:, one], 1.0 / D, 1e-6, ALU.mult, ALU.add).then_inc(s_var, 1)
                v.wait_ge(s_std, n + 1)
                own_.up(v.reciprocal(rstd[:, one], std[:, one]))
                own_.settle()
                if ln:
                    own_.up(v.tensor_scalar(tt[:, b, :], tt[:, b, :], mu[:, one], rstd[:, one], ALU.subtract, ALU.mult))
                    own_.settle()
                    own_.up(v.tensor_tensor(tt[:, b, :], tt[:, b, :], gain[:], ALU.mult))
                    own_.settle()
                    v.tensor_tensor(tt[:, b, :], tt[:, b, :], offset[:], ALU.add).then_inc(s_res[b], 1)
                else:
                    own_.up(v.scalar_tensor_tensor(tt[:, b, :], pY[:, b, :], rstd[:, one], gate_row[:],
                                                   ALU.mult, ALU.mult))
                    own_.settle()
                    v.tensor_tensor(tt[:, b, :], tt[:, b, :], xg[:, b, :], ALU.add).then_inc(s_res[b], 1)
            if ln:
                v.wait_ge(s_c, 32)
            skeleton(v, ((1, low), (-1, finish), (2, gate)), own_, 2 * (1 + 5) if ln else 2 * (1 + 2))


def stage_turn(nc, used, rows, meta, hT):
    hT_hi, hT_lo = hT
    NB = 4
    with ExitStack() as own:
        m = Memory(nc, own, used)
        ident = m.sb("identT", [P, P])
        xt = m.sb("xtT", [P, NB, D])
        mt = m.sb("metaT", [NMETA, D])
        pT = m.ps("pTT", [P, NB, D])
        s_x = [m.sem(f"t_rows_loaded{j}") for j in range(NB)]
        s_tr = [m.sem(f"t_turned{j}") for j in range(NB)]
        s_hi = m.sem("t_high")
        s_lo = [m.sem(f"t_low{j}") for j in range(NB)]
        s_m, s_const, s_gp = m.sem("t_meta_loaded"), m.sem("t_identity"), m.sem("t_pool_own")
        s_mt, s_mh, s_ml = m.sem("t_meta_turned"), m.sem("t_meta_high"), m.sem("t_meta_low")
        block = own.enter_context(nc.Block())

        @block.sync
        def _(sp):
            sp.dma_start(mt[:], meta[:, :]).then_inc(s_m, 16)
            with sp.Fori(0, NT // NB) as i:
                for j in range(NB):
                    sp.wait_ge(s_tr[j], i)
                    sp.dma_start(xt[:, j, :], rows[ds(i * (NB * P) + j * P, P), :]).then_inc(s_x[j], 16)

        @block.gpsimd
        def _(gp):
            own_ = Tally(gp, s_gp)
            own_.up(gp.memset(ident[:], 0.0))
            own_.settle()
            gp.affine_select(out=ident[:], in_=ident[:], compare_op=ALU.not_equal, fill=1.0, base=0,
                             pattern=[[-1, P]], channel_multiplier=1).then_inc(s_const, 1)

        @block.tensor
        def _(pe):
            pe.wait_ge(s_const, 1)
            pe.wait_ge(s_m, 16)
            for k in range(DC):
                last = pe.transpose(pT[:, NB - 1, k * NMETA:(k + 1) * NMETA], mt[:, k * P:(k + 1) * P],
                                    ident[0:NMETA, 0:NMETA])
            last.then_inc(s_mt, 1)
            pe.wait_ge(s_ml, 1)
            with pe.Fori(0, NT // NB) as i:
                for j in range(NB):
                    pe.wait_ge(s_x[j], i * 16 + 16)
                    pe.wait_ge(s_lo[j], i)
                    for k in range(DC):
                        last = pe.transpose(pT[:, j, k * P:(k + 1) * P], xt[:, j, k * P:(k + 1) * P], ident[:])
                    last.then_inc(s_tr[j], 1)

        @block.scalar
        def _(act):
            act.wait_ge(s_mt, 1)
            act.activation(hT_hi[:, :, S:E], pT[:, NB - 1, 0:DC * NMETA].rearrange("p (k r) -> p k r", k=DC),
                           ACT.Copy).then_inc(s_mh, 1)
            with act.Fori(0, NT // NB) as i:
                for j in range(NB):
                    act.wait_ge(s_tr[j], i + 1)
                    act.activation(hT_hi[:, :, ds(i * (NB * P) + j * P, P)],
                                   pT[:, j, :].rearrange("p (k r) -> p k r", k=DC), ACT.Copy).then_inc(s_hi, 1)

        @block.vector
        def _(v):
            v.wait_ge(s_mh, 1)
            v.tensor_tensor(hT_lo[:, :, S:E], pT[:, NB - 1, 0:DC * NMETA].rearrange("p (k r) -> p k r", k=DC),
                            hT_hi[:, :, S:E].bitcast(F32), ALU.subtract).then_inc(s_ml, 1)
            with v.Fori(0, NT // NB) as i:
                for j in range(NB):
                    at = ds(i * (NB * P) + j * P, P)
                    v.wait_ge(s_hi, i * NB + j + 1)
                    v.tensor_tensor(hT_lo[:, :, at], pT[:, j, :].rearrange("p (k r) -> p k r", k=DC),
                                    hT_hi[:, :, at].bitcast(F32), ALU.subtract).then_inc(s_lo[j], 1)


GH, GD = 4, 128
LEVELS = [64, 32, 16, 8, 4, 2, 1]


def stage_recur(nc, used, QH, FH, FHm, IV, IVm, lb_raw, norm_g, RR):
    NI = 2 + len(LEVELS)
    NL = len(LEVELS)
    NG = NT // 4
    with ExitStack() as own:
        m = Memory(nc, own, used)
        ident = m.sb("identG", [P, P])
        sel = m.sb("selG", [P, 1 + NL, P], I32)
        self_ = m.sb("selfG", [P, P])
        raw_f, raw_q = m.sb("raw_fG", [P, E]), m.sb("raw_qG", [P, S])
        F, kf, b = m.sb("FG", [P, E]), m.sb("kfG", [P, E]), m.sb("bG", [P, E])
        sq, qf = m.sb("sqG", [P, S]), m.sb("qfG", [P, S])
        reset = m.sb("resetG", [P, E], BF16)
        X = m.sb("XG", [P, 3, E])
        Z = [m.sb(f"ZG{j}", [P, S]) for j in range(3)]
        Kd, QE = m.sb("KdG", [P, E]), m.sb("QEG", [P, S])
        KdT, KdTm = m.sb("KdTG", [P, NT, P]), m.sb("KdTmG", [NMETA, P])
        AT = m.sb("ATG", [P, NT, P])
        St = m.sb("StG", [P, NT + 1, P])
        Dl = m.sb("DlG", [P, NT])
        V, Vm = m.sb("VG", [P, NT, P]), m.sb("VmG", [NMETA, P])
        O = m.sb("OG", [P, NT, P])
        ssq, var, std, rstd = (m.sb(n, [P, NT]) for n in ("ssqG", "varG", "stdG", "rstdG"))
        gn = m.sb("gnG", [P, P])
        lraw, lexp, linv, lp, lb, oml = (m.sb(n, [P, GH]) for n in ("lraw", "lexp", "linv", "lp", "lbG", "omlG"))
        pG = m.ps("pGG", [P, 4, 4, P])
        pX = m.ps("pXG", [P, 2, 4, P])
        pM = m.ps("pMG", [P, 2, 512])

        s_c = m.sem("g_vectors_loaded")
        s_rq, s_v = m.sem("g_qf_loaded"), m.sem("g_values_loaded")
        s_const, s_gp, s_dve, s_act = (m.sem("g_" + n) for n in ("constants", "pool_own", "dve_own", "act_own"))
        s_lb0, s_lb1, s_lb = m.sem("g_lb_zeroed"), m.sem("g_lb_exp"), m.sem("g_lb_made")
        s_sig, s_sq = m.sem("g_sigmoid_f"), m.sem("g_sigmoid_q")
        s_f, s_g, s_b = m.sem("g_f_made"), m.sem("g_log_f"), m.sem("g_b_made")
        s_qk = m.sem("g_q_made")
        s_D = m.sem("g_chunk_decay")
        s_x, s_e, s_z = m.sem("g_difference"), m.sem("g_decay"), m.sem("g_decayed")
        s_lv = [m.sem(f"g_level_product{k}") for k in range(4)]
        s_pc = [m.sem(f"g_level_copied{k}") for k in range(4)]
        s_px = [m.sem(f"g_product{k}") for k in range(2)]
        s_xf = [m.sem(f"g_product_used{k}") for k in range(2)]
        s_mt, s_mc, s_mu, s_m0 = (m.sem("g_meta_" + n) for n in ("turned", "copied", "product", "state"))
        s_O = m.sem("g_o_squared")
        s_var, s_std = m.sem("g_var"), m.sem("g_root")
        s_on = m.sem("g_o_scaled")
        s_tick = [m.sem(f"g_tick{j}") for j in range(2)]
        s_res, s_st = m.sem("g_result"), m.sem("g_stored")

        TURN, UPD, OUT = 0, 4, 8

        block = own.enter_context(nc.Block())

        @block.sync
        def _(sp):
            with nc.allow_non_contiguous_dma(reason="a vector of 2 KB"):
                sp.dma_start(lraw[:], lb_raw.rearrange("a (k p) -> p (a k)", p=P)).then_inc(s_c, 16)
            sp.dma_start(gn[:], norm_g.to_broadcast([P, P])).then_inc(s_c, 16)
            with sp.Fori(0, GH) as h:
                sp.wait_ge(s_qk, h)
                sp.sem_inc(s_tick[0], 1)
                sp.dma_start(raw_f[:, 0:S], FH[ds(h * GD, GD), :]).then_inc(s_rq, 16)
                sp.dma_start(raw_f[:, S:E], FHm[ds(h * GD, GD), :]).then_inc(s_rq, 16)
                sp.dma_start(raw_q[:], QH[ds(h * GD, GD), :]).then_inc(s_rq, 16)
                sp.wait_ge(s_O, h)
                sp.sem_inc(s_tick[0], 1)
                sp.dma_start(V[:], IV[:, ds(h * GD, GD)].rearrange("(t p) d -> p t d", p=P)).then_inc(s_v, 16)
                sp.dma_start(Vm[:], IVm[:, ds(h * GD, GD)]).then_inc(s_v, 16)

        @block.gpsimd
        def _(gp):
            own_ = Tally(gp, s_gp)
            own_.up(gp.memset(ident[:], 0.0))
            own_.up(gp.memset(AT[:], 0.0))
            own_.up(gp.memset(reset[:], 1.0))
            own_.settle()
            own_.up(gp.memset(reset[:, 0:S].rearrange("p (c k) -> p c k", k=P)[:, :, 0:1], 0.0))
            own_.up(gp.memset(reset[:, S:S + 1], 0.0))
            own_.up(gp.affine_select(out=ident[:], in_=ident[:], compare_op=ALU.not_equal, fill=1.0, base=0,
                                     pattern=[[-1, P]], channel_multiplier=1))
            own_.settle()
            own_.up(gp.tensor_copy(sel[:, 0, :], ident[:]))
            for l, w in enumerate(LEVELS):
                own_.up(gp.memset(self_[:], 0.0))
                own_.settle()
                for blk in range(P // (2 * w)):
                    own_.up(gp.memset(self_[:, blk * 2 * w + w:(blk + 1) * 2 * w], 1.0))
                own_.settle()
                view = self_[:].rearrange("p (n z) -> p n z", z=2 * w)
                nb = P // (2 * w)
                own_.up(gp.affine_select(out=view, in_=view, compare_op=ALU.is_ge, fill=0.0, base=0,
                                         pattern=[[-2 * w, nb], [0, 2 * w]], channel_multiplier=1))
                own_.settle()
                own_.up(gp.affine_select(out=view, in_=view, compare_op=ALU.is_gt, fill=0.0, base=w,
                                         pattern=[[2 * w, nb], [0, 2 * w]], channel_multiplier=-1))
                own_.settle()
                own_.up(gp.tensor_copy(sel[:, 1 + l, :], self_[:]))
                own_.settle()
            gp.sem_inc(s_const, 1)

            with gp.Fori(0, GH) as h:
                for j in range(NI):
                    gp.wait_ge(s_e, h * NI + j + 1)
                    if j >= 2:
                        l = j - 2
                        if l < 3:
                            for k in range(4):
                                gp.wait_ge(s_lv[k], h * (NL + 1))
                        else:
                            gp.wait_ge(s_lv[3], h * (NL + 1) + (l - 3) + 2)
                        w = LEVELS[l]
                        vw = lambda t: t.rearrange("p (n z k) -> p n z k", z=2, k=w)
                        x, z = vw(X[:, j % 3, 0:S]), vw(Z[j % 3][:])
                        gp.tensor_tensor(z[:, :, 0, :], vw(kf[:, 0:S])[:, :, 0, :], x[:, :, 0, :], ALU.mult
                                         ).then_inc(s_gp, 1)
                        gp.tensor_tensor(z[:, :, 1, :], vw(qf[:])[:, :, 1, :], x[:, :, 1, :], ALU.mult
                                         ).then_inc(s_z, 1)
                    elif j == 0:
                        for k in range(2):
                            gp.wait_ge(s_xf[k], h * 6)
                        gp.tensor_tensor(Kd[:], kf[:], X[:, 0, :], ALU.mult).then_inc(s_z, 1)
                    else:
                        gp.tensor_tensor(QE[:], qf[:], X[:, 1, 0:S], ALU.mult).then_inc(s_z, 1)
                gp.wait_ge(s_on, h + 1)
                gp.tensor_tensor(O[:], O[:], gn[:].unsqueeze(1).to_broadcast([P, NT, P]), ALU.mult).then_inc(s_res, 1)
                gp.wait_ge(s_res, h + 1)
                gp.dma_start(RR[:, ds(h * GD, GD)].rearrange("(t p) d -> p t d", p=P), O[:]).then_inc(s_st, 16)
            gp.wait_ge(s_st, 16 * GH)

        @block.scalar
        def _(act):
            act.wait_ge(s_lb0, 1)
            act.activation(lexp[:], lp[:], ACT.Exp).then_inc(s_lb1, 1)
            with act.Fori(0, GH) as h:
                act.wait_ge(s_rq, h * 48 + 48)
                act.activation(F[:], raw_f[:], ACT.Sigmoid).then_inc(s_sig, 1)
                act.activation(sq[:], raw_q[:], ACT.Sigmoid).then_inc(s_sq, 1)
                act.wait_ge(s_f, h + 1)
                act.activation(F[:], F[:], ACT.Ln).then_inc(s_g, 1)
                act.wait_ge(s_b, h + 1)
                act.activation(Dl[:], b[:, 0:S].rearrange("p (c k) -> p c k", k=P)[:, :, P - 1], ACT.Exp
                               ).then_inc(s_D, 1)

                def product_out(e, dst):
                    k = e % 2
                    act.wait_ge(s_px[k], h * 6 + e // 2 + 1)
                    act.activation(dst, pX[:, k], ACT.Copy).then_inc(s_xf[k], 1)

                for j in range(NI):
                    act.wait_ge(s_x, h * NI + j + 1)
                    at = slice(0, E) if j == 0 else slice(0, S)
                    act.activation(X[:, j % 3, at], X[:, j % 3, at], ACT.Exp).then_inc(s_e, 1)
                    if j == 3:
                        for e in range(TURN, TURN + NG):
                            product_out(e, KdT[:, 4 * e:4 * e + 4, :])
                        act.wait_ge(s_mt, h + 1)
                        act.activation(KdTm[:], pM[0:NMETA, 0, 0:P], ACT.Copy).then_inc(s_mc, 1)
                act.wait_ge(s_st, h * 16)
                for e in range(OUT, OUT + NG):
                    product_out(e, O[:, 4 * (e - OUT):4 * (e - OUT) + 4, :])
                act.wait_ge(s_xf[0], h * 6 + 6)
                act.wait_ge(s_xf[1], h * 6 + 6)
                act.activation(sq[:], O[:].rearrange("p t d -> p (t d)"), ACT.Square).then_inc(s_O, 1)
                act.wait_ge(s_var, h + 1)
                act.activation(std[:], var[:], ACT.Sqrt).then_inc(s_std, 1)

        @block.vector
        def _(v):
            own_ = Tally(v, s_dve)
            v.wait_ge(s_c, 32)
            v.tensor_tensor(lp[:], lraw[:], lraw[:], ALU.subtract).then_inc(s_lb0, 1)
            v.wait_ge(s_lb1, 1)
            own_.up(v.reciprocal(linv[:], lexp[:]))
            own_.settle()
            own_.up(v.tensor_tensor(lp[:], lexp[:], linv[:], ALU.mult))
            own_.settle()
            own_.up(v.tensor_tensor(lb[:], lp[:], lp[:], ALU.subtract))
            own_.settle()
            own_.up(v.tensor_scalar(oml[:], lb[:], -1.0, 1.0, ALU.mult, ALU.add))
            own_.settle()
            v.wait_ge(s_const, 1)
            PER = 1 + 1 + NL + (NT - NG) + 2
            with v.Fori(0, GH) as h:
                own_.enter(h, PER)
                col = ds(h, 1)
                v.wait_ge(s_sig, h + 1)
                own_.up(v.tensor_scalar(F[:], F[:], oml[:, col], lb[:, col], ALU.mult, ALU.add))
                own_.settle()
                v.tensor_scalar(kf[:], F[:], -1.0, 1.0, ALU.mult, ALU.add).then_inc(s_f, 1)
                v.wait_ge(s_sq, h + 1)
                v.scalar_tensor_tensor(qf[:], raw_q[:], GD ** -0.5, sq[:], ALU.mult, ALU.mult).then_inc(s_qk, 1)
                v.wait_ge(s_g, h + 1)
                v.tensor_tensor_scan(b[:], reset[:], F[:], 0.0, ALU.mult, ALU.add).then_inc(s_b, 1)
                v.wait_ge(s_b, h + 1)

                def difference(j):
                    v.wait_ge(s_z, h * NI + max(0, j - 2))
                    x = X[:, j % 3, :]
                    if j == 0:
                        c3 = lambda t: t[:, 0:S].rearrange("p (c k) -> p c k", k=P)
                        own_.up(v.tensor_tensor(c3(x), c3(b)[:, :, P - 1:P].to_broadcast([P, NT, P]), c3(b),
                                                ALU.subtract))
                        v.tensor_tensor(x[:, S:E], b[:, E - 1:E].to_broadcast([P, NMETA]), b[:, S:E], ALU.subtract
                                        ).then_inc(s_x, 1)
                    elif j == 1:
                        v.tensor_copy(x[:, 0:S], b[:, 0:S]).then_inc(s_x, 1)
                    else:
                        w = LEVELS[j - 2]
                        vw = lambda t: t.rearrange("p (n z k) -> p n z k", z=2, k=w)
                        xb, bb = vw(x[:, 0:S]), vw(b[:, 0:S])
                        ref = bb[:, :, 0, w - 1:w].to_broadcast([P, S // (2 * w), w])
                        own_.up(v.tensor_tensor(xb[:, :, 0, :], ref, bb[:, :, 0, :], ALU.subtract))
                        v.tensor_tensor(xb[:, :, 1, :], bb[:, :, 1, :], ref, ALU.subtract).then_inc(s_x, 1)

                def level(l):
                    for k in range(NG):
                        v.wait_ge(s_lv[k], h * (NL + 1) + l + 1)
                        v.sem_inc(s_tick[1], 1)
                        v.copy_predicated(AT[:, 4 * k:4 * k + 4, :],
                                          sel[:, l:l + 1, :].to_broadcast([P, 4, P]), pG[:, k]).then_inc(s_pc[k], 1)

                for j in range(3):
                    difference(j)
                level(0)
                difference(3)
                v.wait_ge(s_mu, h + 1)
                v.tensor_copy(St[:, 0, :], pM[:, 1, 0:P]).then_inc(s_m0, 1)
                v.wait_ge(s_m0, h + 1)
                v.wait_ge(s_D, h + 1)
                for c in range(NT):
                    e = UPD + c // 4
                    if c % 4 == 0:
                        v.wait_ge(s_px[e % 2], h * 6 + e // 2 + 1)
                    ins = v.scalar_tensor_tensor(St[:, c + 1, :], St[:, c, :], Dl[:, c:c + 1], pX[:, e % 2, c % 4, :],
                                                 ALU.mult, ALU.add)
                    if c % 4 == 3:
                        ins.then_inc(s_xf[e % 2], 1)
                        v.wait_ge(s_xf[e % 2], h * 6 + e // 2 + 1)
                    else:
                        own_.up(ins)
                        own_.settle()
                for l in range(1, NL + 1):
                    level(l)
                    if l + 3 < NI:
                        difference(l + 3)
                v.wait_ge(s_O, h + 1)
                own_.up(v.tensor_reduce(ssq[:], sq[:].rearrange("p (t d) -> p t d", d=P), AX.X, ALU.add))
                own_.settle()
                v.tensor_scalar(var[:], ssq[:], 1.0 / GD, 1e-6, ALU.mult, ALU.add).then_inc(s_var, 1)
                v.wait_ge(s_std, h + 1)
                own_.up(v.reciprocal(rstd[:], std[:]))
                own_.settle()
                v.tensor_tensor(O[:], O[:], rstd[:].unsqueeze(2).to_broadcast([P, NT, P]), ALU.mult).then_inc(s_on, 1)
                own_.leave(GH)

        @block.tensor
        def _(pe):
            pe.wait_ge(s_const, 1)
            with pe.Fori(0, GH) as h:
                def level(l, lhsT, rhs):
                    for k in range(NG):
                        pe.wait_ge(s_pc[k], h * (NL + 1) + l)
                        for c in range(4):
                            at = slice((4 * k + c) * P, (4 * k + c + 1) * P)
                            last = pe.matmul(pG[:, k, c, :], lhsT=lhsT[:, at], rhs=rhs[:, at], start=True, stop=True)
                        last.then_inc(s_lv[k], 1)

                def group(e, make):
                    k = e % 2
                    pe.wait_ge(s_xf[k], h * 6 + e // 2)
                    for c in range(4):
                        last = make(k, 4 * (e % 4) + c, c)
                    last.then_inc(s_px[k], 1)

                pe.wait_ge(s_qk, h + 1)
                pe.wait_ge(s_f, h + 1)
                level(0, kf, qf)
                pe.wait_ge(s_z, h * NI + 1)
                for e in range(TURN, TURN + NG):
                    group(e, lambda k, t, c: pe.transpose(pX[:, k, c, :], Kd[:, t * P:(t + 1) * P], ident[:]))
                pe.wait_ge(s_mc, h)
                pe.transpose(pM[0:NMETA, 0, 0:P], Kd[:, S:E], ident[:]).then_inc(s_mt, 1)
                pe.wait_ge(s_mc, h + 1)
                pe.wait_ge(s_v, h * 32 + 32)
                pe.wait_ge(s_m0, h)
                pe.matmul(pM[:, 1, 0:P], lhsT=KdTm[:], rhs=Vm[:], start=True, stop=True).then_inc(s_mu, 1)
                for e in range(UPD, UPD + NG):
                    group(e, lambda k, t, c: pe.matmul(pX[:, k, c, :], lhsT=KdT[:, t, :], rhs=V[:, t, :],
                                                       start=True, stop=True))
                for l in range(1, NL + 1):
                    j = l + 1
                    pe.wait_ge(s_z, h * NI + j + 1)
                    level(l, Z[j % 3], Z[j % 3])
                for k in range(4):
                    pe.wait_ge(s_pc[k], h * (NL + 1) + NL + 1)

                def out(k, t, c):
                    pe.matmul(pX[:, k, c, :], lhsT=QE[:, t * P:(t + 1) * P], rhs=St[:, t, :], start=True, stop=False)
                    return pe.matmul(pX[:, k, c, :], lhsT=AT[:, t, :], rhs=V[:, t, :], start=False, stop=True)
                for e in range(OUT, OUT + NG):
                    group(e, out)


IH, ID = 4, 64
TOPK = 256
OFF = [P * i * (i + 1) // 2 for i in range(NT + 1)]


def stage_select(nc, used, QI, KI, WI, MK):
    CH = 512
    FREE = TOPK // P
    NQ = NT - FREE
    chunks = {i: -(-(i + 1) * P // CH) for i in range(FREE, NT)}
    before = {i: sum(chunks[j] for j in range(FREE, i)) for i in range(FREE, NT)}
    BASE = OFF[FREE]
    BY_ACT = (15, 14, 13, 10, 7, 4)
    BITS = 32
    with ExitStack() as own:
        m = Memory(nc, own, used)
        ident, causal = m.sb("identI", [P, P]), m.sb("causalI", [P, P])
        k_raw = m.sb("krawI", [P, S])
        k_high, k_parts = m.sb("khighI", [P, S], F32R), m.sb("kpartsI", [P, S], F32R)
        q_raw = m.sb("qrawI", [P, 2, IH, P])
        q_high, q_low = (m.sb(n, [P, 2, IH, P], F32R) for n in ("qhighI", "qlowI"))
        w = m.sb("wI", [P, NT, IH])
        wh = m.sb("whI", [P, NT, IH])
        rl = m.sb("rlI", [P, 2, IH, CH])
        x = m.sb("xI", [P, OFF[NT] - BASE])
        key, bit, cand, low, mask = (m.sb(n + "I", [P, NQ], I32) for n in ("key", "bit", "cand", "low", "msk"))
        ones = m.sb("onesbI", [P, NQ], I32)
        T, bias, count, want, quota = (m.sb(n + "I", [P, NQ]) for n in ("T", "bias", "count", "want", "quota"))
        junk = m.sb("junkI", [P, OFF[NT] - BASE], BF16)
        one_row = m.sb("onerowI", [P, S], BF16)
        eq, rank = m.sb("eqI", [P, S]), m.sb("rankI", [P, S])
        mk = m.sb("mkI", [P, 2, S], BF16)
        pS = m.ps("pSI", [P, 2, IH, CH])
        s_in, s_const, s_gp, s_dve = (m.sem("i_" + n) for n in ("loaded", "constants", "pool_own", "dve_own"))
        s_kin, s_ksplit, s_qsplit = m.sem("i_keys_loaded"), m.sem("i_keys_split"), m.sem("i_queries_split")
        s_qin = [m.sem(f"i_queries_loaded{b}") for b in range(2)]
        s_sc, s_rl, s_add = m.sem("i_scores"), m.sem("i_relu"), m.sem("i_added")
        s_cand, s_counted = m.sem("i_candidates"), m.sem("i_signs_summed")
        s_mk = m.sem("i_mask")
        s_st = [m.sem(f"i_stored{b}") for b in range(2)]
        s_tick = m.sem("i_tick")

        def scores(i):
            return x[:, OFF[i] - BASE:OFF[i + 1] - BASE]

        def thrown(i):
            return junk[:, OFF[i] - BASE:OFF[i + 1] - BASE]

        block = own.enter_context(nc.Block())

        @block.sync
        def _(sp):
            with nc.allow_non_contiguous_dma(reason="index weights, 16 bytes a row"):
                sp.dma_start(w[:], WI.rearrange("(t p) h -> p t h", p=P)).then_inc(s_in, 16)
            sp.dma_start(k_raw[:], KI[:, :]).then_inc(s_kin, 16)
            for i in range(FREE, NT):
                b = i % 2
                if i - FREE >= 2:
                    sp.wait_ge(s_qsplit, 2 * (i - FREE - 2) + 2)
                for half in range(2):
                    sp.dma_start(q_raw[half * ID:(half + 1) * ID, b],
                                 QI.rearrange("(h d) t -> d h t", d=ID)[:, :, i * P:(i + 1) * P]).then_inc(s_qin[b], 16)
            for i in range(NT):
                sp.wait_ge(s_mk, i + 1)
                n = (i + 1) * P
                sp.dma_start(MK[:, OFF[i]:OFF[i] + n], mk[:, i % 2, 0:n]).then_inc(s_st[i % 2], 16)
            for b in range(2):
                sp.wait_ge(s_st[b], 16 * NT // 2)

        @block.gpsimd
        def _(gp):
            own_ = Tally(gp, s_gp)
            make_masks(gp, own_, ident[:], causal[:])
            own_.up(gp.memset(one_row[:], 1.0))
            own_.settle()
            gp.sem_inc(s_const, 1)
            lower, upper = slice(0, ID), slice(ID, P)
            gp.wait_ge(s_kin, 16)
            gp.tensor_copy(k_parts[lower], k_raw[lower]).then_inc(s_ksplit, 1)
            gp.wait_ge(s_ksplit, 1)
            gp.tensor_copy(k_high[upper], k_raw[upper]).then_inc(s_ksplit, 1)
            gp.wait_ge(s_ksplit, 2)
            gp.tensor_tensor(k_parts[upper], k_raw[upper], k_high[upper].bitcast(F32), ALU.subtract
                             ).then_inc(s_ksplit, 1)
            gp.wait_ge(s_ksplit, 3)
            for i in range(FREE, NT):
                b, n = i % 2, i - FREE
                gp.wait_ge(s_qin[b], 32 * (n // 2) + 32)
                if n >= 2:
                    gp.wait_ge(s_sc, before[i - 1])
                gp.tensor_copy(q_high[:, b], q_raw[:, b]).then_inc(s_qsplit, 1)
                gp.wait_ge(s_qsplit, 2 * n + 1)
                gp.tensor_tensor(q_low[lower, b], q_raw[lower, b], q_high[lower, b].bitcast(F32), ALU.subtract
                                 ).then_inc(s_qsplit, 1)
                gp.wait_ge(s_qsplit, 2 * n + 2)

        @block.tensor
        def _(pe):
            pe.wait_ge(s_ksplit, 3)
            for i in range(FREE, NT):
                pe.wait_ge(s_qsplit, 2 * (i - FREE) + 2)
                for c in range(chunks[i]):
                    g = before[i] + c
                    wd = min(CH, (i + 1) * P - c * CH)
                    if g >= 2:
                        pe.wait_ge(s_rl, g - 1)
                    keys = slice(c * CH, c * CH + wd)
                    for h in range(IH):
                        pe.matmul(pS[:, g % 2, h, 0:wd], lhsT=q_high[:, i % 2, h, :], rhs=k_parts[:, keys],
                                  start=True, stop=False)
                        last = pe.matmul(pS[:, g % 2, h, 0:wd], lhsT=q_low[0:ID, i % 2, h, :],
                                         rhs=k_parts[0:ID, keys], start=False, stop=True)
                    last.then_inc(s_sc, 1)

        @block.scalar
        def _(act):
            for i in range(FREE, NT):
                for c in range(chunks[i]):
                    g = before[i] + c
                    wd = min(CH, (i + 1) * P - c * CH)
                    act.wait_ge(s_sc, g + 1)
                    if g >= 2:
                        act.wait_ge(s_add, g - 1)
                    act.activation(rl[:, g % 2, :, 0:wd], pS[:, g % 2, :, 0:wd], ACT.Relu, scale=0.125).then_inc(s_rl, 1)


            with act.Fori(0, BITS) as r:
                act.wait_ge(s_cand, r + 1)
                for z, i in enumerate(BY_ACT):
                    j = i - FREE
                    last = act.activation(thrown(i), scores(i), ACT.Sign, bias=bias[:, j:j + 1],
                                          accum_out=count[:, j:j + 1])
                last.then_inc(s_counted, 1)

        @block.vector
        def _(v):
            own_ = Tally(v, s_dve)

            def step(ins):
                own_.up(ins)
                own_.settle()
            v.wait_ge(s_in, 16)
            own_.up(v.memset(key[:], 0))
            own_.up(v.memset(ones[:], -1))
            own_.up(v.memset(bit[:], -2**31))
            for i in range(FREE, NT):
                last = v.memset(want[:, i - FREE:i - FREE + 1], float(2 * TOPK - (i + 1) * P if i in BY_ACT else TOPK))
            own_.up(last)
            step(v.tensor_scalar(wh[:], w[:], 0.5, None, ALU.mult))
            v.wait_ge(s_const, 1)
            for i in range(FREE):
                if i:
                    v.memset(mk[:, i, 0:i * P], 0.0)
                v.tensor_copy(mk[:, i, i * P:(i + 1) * P], causal[:]).then_inc(s_mk, 1)
            for i in range(FREE, NT):
                n = (i + 1) * P
                to = scores(i)
                for c in range(chunks[i]):
                    g = before[i] + c
                    wd = min(CH, n - c * CH)
                    at = slice(c * CH, c * CH + wd)
                    v.wait_ge(s_rl, g + 1)
                    step(v.tensor_scalar(to[:, at], rl[:, g % 2, 0, 0:wd], wh[:, i, 0:1], None, ALU.mult))
                    for h in range(1, IH):
                        ins = v.scalar_tensor_tensor(to[:, at], rl[:, g % 2, h, 0:wd], wh[:, i, h:h + 1],
                                                     to[:, at], ALU.mult, ALU.add)
                        if h < IH - 1:
                            step(ins)
                        else:
                            ins.then_inc(s_add, 1)
                            v.wait_ge(s_add, g + 1)
                step(v.tensor_tensor(to[:, i * P:n], to[:, i * P:n], causal[:], ALU.add))

            def as_float(key_, to):
                step(v.tensor_scalar(low[:], key_, 31, 1, ALU.arith_shift_right, ALU.logical_shift_right))
                step(v.tensor_tensor(low[:], key_, low[:], ALU.bitwise_xor))
                step(v.tensor_tensor(to, low[:], ones[:], ALU.bitwise_xor))

            with v.Fori(0, BITS) as r:
                own_.enter(r, 10)
                step(v.tensor_tensor(cand[:], key[:], bit[:], ALU.bitwise_or))
                as_float(cand[:], T[:].bitcast(I32))
                v.tensor_scalar(bias[:], T[:], -1.0, None, ALU.mult).then_inc(s_cand, 1)
                for i in range(FREE, NT):
                    if i not in BY_ACT:
                        j = i - FREE
                        last = v.tensor_scalar(thrown(i), scores(i), T[:, j:j + 1], None, ALU.is_ge,
                                               ALU.add, accum_out=count[:, j:j + 1])
                own_.up(last)
                v.wait_ge(s_counted, r + 1)
                v.sem_inc(s_tick, 1)
                own_.settle()
                step(v.tensor_tensor(mask[:], count[:], want[:], ALU.is_ge))
                step(v.tensor_scalar(mask[:], mask[:], 31, 31, ALU.logical_shift_left, ALU.arith_shift_right))
                step(v.tensor_tensor(mask[:], mask[:], bit[:], ALU.bitwise_and))
                step(v.tensor_tensor(key[:], key[:], mask[:], ALU.bitwise_or))
                step(v.tensor_scalar(bit[:], bit[:], 1, None, ALU.logical_shift_right))
                own_.leave(BITS)

            def count_above():
                for i in range(FREE, NT):
                    j = i - FREE
                    last = v.tensor_scalar(thrown(i), scores(i), T[:, j:j + 1], None, ALU.is_gt,
                                           ALU.add, accum_out=count[:, j:j + 1])
                step(last)
            as_float(key[:], T[:].bitcast(I32))
            count_above()
            step(v.tensor_scalar(mask[:], count[:], float(TOPK), None, ALU.is_ge))
            step(v.tensor_scalar(low[:], key[:], 16, 16, ALU.logical_shift_left, ALU.logical_shift_right))
            step(v.tensor_tensor(low[:], low[:], mask[:], ALU.add))
            step(v.tensor_scalar(cand[:], key[:], 16, None, ALU.logical_shift_right))
            step(v.tensor_scalar(mask[:], low[:], 16, None, ALU.logical_shift_right))
            step(v.tensor_tensor(cand[:], cand[:], mask[:], ALU.add))
            step(v.tensor_scalar(cand[:], cand[:], 16, None, ALU.logical_shift_left))
            step(v.tensor_scalar(low[:], low[:], 16, 16, ALU.logical_shift_left, ALU.logical_shift_right))
            step(v.tensor_tensor(key[:], cand[:], low[:], ALU.bitwise_or))
            as_float(key[:], T[:].bitcast(I32))
            count_above()
            step(v.tensor_scalar(quota[:], count[:], -1.0, float(TOPK), ALU.mult, ALU.add))
            for i in range(FREE, NT):
                b, n, j = i % 2, (i + 1) * P, i - FREE
                one = slice(j, j + 1)
                v.wait_ge(s_st[b], 16 * (i // 2))
                v.wait_ge(s_mk, i)
                step(v.tensor_scalar(eq[:, 0:n], scores(i), T[:, one], None, ALU.is_equal))
                step(v.tensor_tensor_scan(rank[:, 0:n], one_row[:, 0:n], eq[:, 0:n], 0.0, ALU.mult, ALU.add))
                step(v.scalar_tensor_tensor(eq[:, 0:n], rank[:, 0:n], quota[:, one], eq[:, 0:n], ALU.is_le, ALU.mult))
                step(v.scalar_tensor_tensor(eq[:, 0:n], scores(i), T[:, one], eq[:, 0:n], ALU.is_gt, ALU.add))
                v.tensor_scalar(mk[:, b, 0:n], eq[:, 0:n], -1.0, -NEG, ALU.add, ALU.mult).then_inc(s_mk, 1)


RANK = 128
BUCKETS = 32
NE = NT + 1
BAND = P + 96 + NMETA
BACK = BAND - P - NMETA
PITCH = 368


def bucket_table():
    exact = BUCKETS // 2
    dist = np.maximum(P + BACK + NMETA - 1 - np.arange(PITCH), 0)
    large = exact + (np.log(np.maximum(dist, 1).astype(np.float32) / np.float32(exact)) / np.float32(np.log(128 / exact))
                     * np.float32(BUCKETS - exact)).astype(np.int32)
    bucket = np.where(dist < exact, dist, np.minimum(large, BUCKETS - 1))
    table = np.zeros((BUCKETS, PITCH), np.float32)
    table[bucket, np.arange(PITCH)] = 1.0
    table[BUCKETS - 1] -= 1.0
    return table


def stage_lift(nc, used, CK, CKm, kv_norm_g, w_uk, w_uv, rel_bias, table, KT, VE, BV):
    with ExitStack() as own:
        m = Memory(nc, own, used)
        ident = m.sb("identL", [P, P])
        c, cn = m.sb("cL", [P, NE, RANK]), m.sb("cnL", [P, NE, RANK])
        sq = m.sb("sqL", [P, NE, RANK])
        ssq, var, std, rstd = (m.sb(n + "L", [P, NE]) for n in ("ssq", "var", "std", "rstd"))
        g = m.sb("gL", [P, RANK])
        uk, ukT = m.sb("ukL", [P, 4, RANK]), m.sb("ukTL", [P, 4, P])
        uv = m.sb("uvL", [P, H, HD])
        cT = m.sb("cTL", [P, E])
        rb, ones, rbB = m.sb("rbL", [BUCKETS, H]), m.sb("onesL", [BUCKETS, P]), m.sb("rbBL", [BUCKETS, H, P])
        tab = m.sb("tabL", [BUCKETS, PITCH])
        bv = m.sb("bvL", [P, 2, PITCH])
        kt = m.sb("ktL", [P, 2, 512])
        ve = m.sb("veL", [P, 2, 512])
        pT = m.ps("pTL", [P, 2, 4, P])
        pK = m.ps("pKL", [P, 2, 512])
        pV = m.ps("pVL", [P, 2, 512])
        pB = m.ps("pBL", [P, 2, 512])
        s_in, s_const, s_gp, s_dve = (m.sem("l_" + n) for n in ("loaded", "constants", "pool_own", "dve_own"))
        s_bv, s_sq, s_std, s_cn = (m.sem("l_" + n) for n in ("bias_columns", "squares", "root", "normalised"))
        s_tr, s_tc = m.sem("l_turned"), m.sem("l_turned_copied")
        s_k, s_v, s_b = m.sem("l_keys"), m.sem("l_values"), m.sem("l_bias")
        s_kc, s_vc, s_bc = m.sem("l_keys_copied"), m.sem("l_values_copied"), m.sem("l_bias_copied")
        s_kst, s_vst, s_bst = ([m.sem(f"l_{n}_stored{b}") for b in range(2)] for n in ("keys", "values", "bias"))
        TURNS = 6
        KEYS = [(j, at, min(512, E - at)) for at in range(0, E, 512) for j in range(4)]

        def latent(t):
            return (NMETA, slice(0, NMETA)) if t == NT else (P, slice(NMETA + t * P, NMETA + (t + 1) * P))

        block = own.enter_context(nc.Block())

        @block.sync
        def _(sp):
            sp.dma_start(c[:, 0:NT, :], CK.rearrange("(t p) d -> p t d", p=P)).then_inc(s_in, 16)
            sp.dma_start(c[0:NMETA, NT, :], CKm[:, :]).then_inc(s_in, 16)
            sp.dma_start(g[:], kv_norm_g.to_broadcast([P, RANK])).then_inc(s_in, 16)
            sp.dma_start(uk[:], w_uk[0].rearrange("h d c -> (h d) c").rearrange("(j p) c -> p j c", p=P)).then_inc(s_in, 16)
            sp.dma_start(uv[:], w_uv[0].rearrange("h c d -> c h d")).then_inc(s_in, 16)
            sp.dma_start(rb[:], rel_bias[:, :]).then_inc(s_in, 16)
            sp.dma_start(tab[:], table[:, :]).then_inc(s_in, 16)
            for h in range(H):
                sp.wait_ge(s_bc, h + 1)
                sp.dma_start(BV[h], bv[:, h % 2]).then_inc(s_bst[h % 2], 16)
            for n, (j, at, w) in enumerate(KEYS):
                sp.wait_ge(s_kc, n + 1)
                sp.dma_start(KT[j * P:(j + 1) * P, at:at + w], kt[:, n % 2, 0:w]).then_inc(s_kst[n % 2], 16)
            for t in range(NE):
                rows, at = latent(t)
                sp.wait_ge(s_vc, t + 1)
                sp.dma_start(VE[at, :], ve[0:rows, t % 2, :]).then_inc(s_vst[t % 2], 16)
            for b in range(2):
                sp.wait_ge(s_kst[b], 16 * ((len(KEYS) + 1 - b) // 2))
                sp.wait_ge(s_vst[b], 16 * ((NE + 1 - b) // 2))
                sp.wait_ge(s_bst[b], 16 * H // 2)

        @block.gpsimd
        def _(gp):
            own_ = Tally(gp, s_gp)
            own_.up(gp.memset(ones[:], 1.0))
            make_masks(gp, own_, ident[:])
            gp.sem_inc(s_const, 1)

        @block.vector
        def _(v):
            own_ = Tally(v, s_dve)
            v.wait_ge(s_in, 7 * 16)
            v.wait_ge(s_const, 1)
            for h in range(H):
                last = v.tensor_scalar(rbB[:, h, :], ones[:], rb[:, h:h + 1], 8.0, ALU.mult, ALU.mult)
            last.then_inc(s_bv, 1)
            for z, lanes in ((slice(0, NT), slice(0, P)), (slice(NT, NE), slice(0, NMETA))):
                own_.up(v.tensor_tensor(sq[lanes, z], c[lanes, z], c[lanes, z], ALU.mult))
                own_.settle()
                own_.up(v.tensor_reduce(ssq[lanes, z], sq[lanes, z], AX.X, ALU.add))
                own_.settle()
                v.tensor_scalar(var[lanes, z], ssq[lanes, z], 1.0 / RANK, 1e-6, ALU.mult, ALU.add).then_inc(s_sq, 1)
            v.wait_ge(s_std, 2)
            for t in range(NE):
                lanes = slice(0, latent(t)[0])
                own_.up(v.reciprocal(rstd[lanes, t:t + 1], std[lanes, t:t + 1]))
            own_.settle()
            for t in range(NE):
                lanes = slice(0, latent(t)[0])
                v.scalar_tensor_tensor(cn[lanes, t], c[lanes, t], rstd[lanes, t:t + 1], g[lanes, :], ALU.mult, ALU.mult
                                       ).then_inc(s_cn, 1)
            for h in range(H):
                v.wait_ge(s_b, h + 1)
                if h >= 2:
                    v.wait_ge(s_bst[h % 2], 16 * (h // 2))
                v.tensor_copy(bv[:, h % 2], pB[:, h % 2, 0:PITCH]).then_inc(s_bc, 1)
            for t in range(NE):
                rows = latent(t)[0]
                v.wait_ge(s_v, t + 1)
                if t >= 2:
                    v.wait_ge(s_vst[t % 2], 16 * (t // 2))
                v.tensor_copy(ve[0:rows, t % 2], pV[0:rows, t % 2]).then_inc(s_vc, 1)

        @block.scalar
        def _(act):
            for z, (cols_, lanes) in enumerate(((slice(0, NT), slice(0, P)), (slice(NT, NE), slice(0, NMETA)))):
                act.wait_ge(s_sq, z + 1)
                act.activation(std[lanes, cols_], var[lanes, cols_], ACT.Sqrt).then_inc(s_std, 1)
            for n in range(TURNS):
                act.wait_ge(s_tr, n + 1)
                if n == 0:
                    act.copy(ukT[:], pT[:, 0]).then_inc(s_tc, 1)
                elif n < TURNS - 1:
                    act.copy(cT[:, NMETA + (n - 1) * 512:NMETA + n * 512], pT[:, n % 2].rearrange("p a b -> p (a b)")
                             ).then_inc(s_tc, 1)
                else:
                    act.copy(cT[:, 0:NMETA], pT[:, n % 2, 0, 0:NMETA]).then_inc(s_tc, 1)
            for n, (j, at, w) in enumerate(KEYS):
                act.wait_ge(s_k, n + 1)
                if n >= 2:
                    act.wait_ge(s_kst[n % 2], 16 * (n // 2))
                act.copy(kt[:, n % 2, 0:w], pK[:, n % 2, 0:w]).then_inc(s_kc, 1)

        @block.tensor
        def _(pe):
            pe.wait_ge(s_const, 1)
            pe.wait_ge(s_in, 7 * 16)
            pe.wait_ge(s_bv, 1)
            for h in range(H):
                if h >= 2:
                    pe.wait_ge(s_bc, h - 1)
                pe.matmul(pB[:, h % 2, 0:PITCH], lhsT=rbB[:, h, :], rhs=tab[:], start=True, stop=True).then_inc(s_b, 1)
            for n in range(TURNS):
                if n >= 2:
                    pe.wait_ge(s_tc, n - 1)
                if n == 0:
                    for j in range(4):
                        last = pe.transpose(pT[:, 0, j], uk[:, j, :], ident[:])
                elif n < TURNS - 1:
                    pe.wait_ge(s_cn, 4 * n)
                    for j in range(4):
                        last = pe.transpose(pT[:, n % 2, j], cn[:, 4 * (n - 1) + j, :], ident[:])
                else:
                    pe.wait_ge(s_cn, NE)
                    last = pe.transpose(pT[:, n % 2, 0, 0:NMETA], cn[0:NMETA, NT, :], ident[0:NMETA, 0:NMETA])
                last.then_inc(s_tr, 1)
            pe.wait_ge(s_tc, TURNS)
            for n, (j, at, w) in enumerate(KEYS):
                if n >= 2:
                    pe.wait_ge(s_kc, n - 1)
                pe.matmul(pK[:, n % 2, 0:w], lhsT=ukT[:, j, :], rhs=cT[:, at:at + w], start=True, stop=True
                          ).then_inc(s_k, 1)
            for t in range(NE):
                rows, at = latent(t)
                if t >= 2:
                    pe.wait_ge(s_vc, t - 1)
                pe.matmul(pV[0:rows, t % 2, :], lhsT=cT[:, at], rhs=uv[:].rearrange("p h d -> p (h d)"),
                          start=True, stop=True).then_inc(s_v, 1)


def stage_latent(nc, used, QAT, KT, VE, BV, MK, AA):
    CH = 512
    seen = [NMETA + (i + 1) * P for i in range(NT)]
    chunks = [-(-n // CH) for n in seen]
    before = [sum(chunks[:i]) for i in range(NT)]
    PER = sum(chunks)
    KR, TR = 4, 2
    with ExitStack() as own:
        m = Memory(nc, own, used)
        ident = m.sb("identN", [P, P])
        ident_r = m.sb("identNr", [P, P], F32R)
        chosen = m.sb("chosenN", [P, OFF[NT] + NT * NMETA], BF16)
        biasf = m.sb("biasN", [P, 2, BAND])
        bias = [m.sb(f"bias{z}N", [P, H, BAND], F32R) for z in range(2)]
        rawq, rawk = m.sb("rawqN", [P, S]), m.sb("rawkN", [P, E])
        kh = m.sb("khN", [P, E], F32R)
        qh, ql, ks, k2 = ([m.sb(f"{n}N{b}", [P, w], F32R) for b in range(2)]
                          for n, w in (("qh", S), ("ql", S), ("ks", E), ("k2", E)))
        vv = m.sb("vvN", [P, 2, NE, HD + 1])
        sc = m.sb("scN", [P, 4, E])
        PT = m.sb("PTN", [P, TR, 4, P])
        mxc = m.sb("mxcN", [P, 2, 5])
        mx, nm = m.sb("mxN", [P, 2]), m.sb("nmN", [P, 4])
        rd = m.sb("rdN", [P, 2])
        oh = m.sb("ohN", [P, 2, NT, HD])
        pS = m.ps("pSN", [P, KR, CH])
        pPT = m.ps("pPTN", [P, TR, 4, P])
        pO = m.ps("pON", [P, 2, 512])

        s_raw = m.sem("n_heads_loaded")
        s_cv = [m.sem(f"n_values_loaded{b}") for b in range(2)]
        s_const = m.sem("n_constants_made")
        s_split = m.sem("n_heads_split")
        s_sc = [m.sem(f"n_scores{k}") for k in range(KR)]
        s_cp = [m.sem(f"n_scores_copied{k}") for k in range(KR)]
        s_nm = m.sem("n_negated_max")
        s_ex = m.sem("n_probabilities")
        s_pt = [m.sem(f"n_probs_transposed{k}") for k in range(TR)]
        s_ptc = [m.sem(f"n_probs_copied{k}") for k in range(TR)]
        s_pv = [m.sem(f"n_values_summed{k}") for k in range(2)]
        s_o = [m.sem(f"n_output_scaled{k}") for k in range(2)]
        s_st = m.sem("n_output_stored")
        s_mk, s_bias = m.sem("n_masks_loaded"), m.sem("n_bias_split")
        s_bl = [m.sem(f"n_bias_loaded{b}") for b in range(2)]
        s_dve = m.sem("n_dve_own")
        s_gp = m.sem("n_pool_own")
        s_tick = m.sem("n_tick")

        def skewed(h):
            flat = BV[h].rearrange("q u -> (q u)")
            return flat[P - 1:P - 1 + P * (PITCH - 1)].rearrange("(q u) -> q u", u=PITCH - 1)[:, 0:BAND]

        block = own.enter_context(nc.Block())

        @block.sync
        def _(sp):
            for i in range(NT):
                sp.dma_start(chosen[:, OFF[i] + (i + 1) * NMETA:OFF[i + 1] + (i + 1) * NMETA],
                             MK[:, OFF[i]:OFF[i + 1]]).then_inc(s_mk, 16)
            for h in range(H):
                if h >= 2:
                    sp.wait_ge(s_bias, 2 * h - 2)
                sp.dma_start(biasf[:, h % 2, :], skewed(h)).then_inc(s_bl[h % 2], 16)

            def load(hd, b, reused):
                sp.wait_ge(s_split, hd * 6)
                for half in range(2):
                    sp.dma_start(rawq[half * HD:(half + 1) * HD, :], QAT[ds(hd * HD, HD), :]).then_inc(s_raw, 16)
                    sp.dma_start(rawk[half * HD:(half + 1) * HD, :], KT[ds(hd * HD, HD), :]
                                 ).then_inc(s_raw, 16)
                if reused:
                    sp.wait_ge(s_pv[1], hd * 8 - 8)
                sp.dma_start(vv[0:NMETA, b, NT, 0:HD], VE[NT * P:E, ds(hd * HD, HD)]).then_inc(s_cv[b], 16)
                sp.dma_start(vv[:, b, 0:NT, 0:HD],
                             VE[0:NT * P, ds(hd * HD, HD)].rearrange("(t p) d -> p t d", p=P)).then_inc(s_cv[b], 16)

            def store(hd, b):
                for k in range(2):
                    sp.wait_ge(s_o[k], hd * 8 + 8)
                sp.dma_start(AA[:, ds(hd * HD, HD)].rearrange("(t p) d -> p t d", p=P), oh[:, b]).then_inc(s_st, 16)

            for b in range(2):
                load(b, b, False)
            with sp.Fori(1, H // 2) as i:
                for b in range(2):
                    load(i * 2 + b, b, True)
                    store(i * 2 + b - 2, b)
            for b in range(2):
                store(H - 2 + b, b)
            sp.wait_ge(s_st, 16 * H)

        @block.gpsimd
        def _(gp):
            own_ = Tally(gp, s_gp)
            make_masks(gp, own_, ident[:])
            gp.tensor_copy(ident_r[:], ident[:]).then_inc(s_const, 1)
            for i in range(NT):
                gp.memset(chosen[:, OFF[i] + i * NMETA:OFF[i] + (i + 1) * NMETA], 0.0).then_inc(s_const, 1)
            gp.memset(vv[:, :, :, HD:HD + 1], 1.0).then_inc(s_const, 1)
            gp.wait_ge(s_const, NT + 2)
            for h in range(H):
                gp.wait_ge(s_bl[h % 2], 16 * (h // 2) + 16)
                gp.tensor_copy(bias[0][:, h, :], biasf[:, h % 2, :]).then_inc(s_bias, 1)
                gp.wait_ge(s_bias, 2 * h + 1)
                gp.tensor_tensor(bias[1][:, h, :], biasf[:, h % 2, :], bias[0][:, h, :].bitcast(F32), ALU.subtract
                                 ).then_inc(s_bias, 1)

            def split(hd, b, reused):
                gp.wait_ge(s_raw, hd * 64 + 64)
                if reused:
                    gp.wait_ge(s_sc[KR - 1], hd * (PER // KR) - PER // KR)
                gp.sem_inc(s_tick, 1)
                lower, upper = slice(0, HD), slice(HD, P)
                steps = ((gp.tensor_copy, qh[b][:], rawq[:]),
                         (gp.tensor_copy, ks[b][lower], rawk[lower]),
                         (gp.tensor_copy, k2[b][lower], rawk[lower]),
                         (gp.tensor_tensor, ql[b][lower], rawq[lower], qh[b][lower].bitcast(F32), ALU.subtract),
                         (gp.tensor_copy, kh[upper], rawk[upper]),
                         (gp.tensor_tensor, ks[b][upper], rawk[upper], kh[upper].bitcast(F32), ALU.subtract))
                for z, (op, *operands) in enumerate(steps):
                    op(*operands).then_inc(s_split, 1)
                    gp.wait_ge(s_split, hd * 6 + (z + 1))
                    gp.sem_inc(s_tick, 1)
            for b in range(2):
                split(b, b, False)
            with gp.Fori(1, H // 2) as i:
                for b in range(2):
                    split(i * 2 + b, b, True)

        STEPS = 2 * NT
        LAG = 2

        def chunk(s, c):
            return (s // NT) * PER + before[s % NT] + c

        def nth(turn, g, ring, per=2 * PER):
            return turn * (per // ring) + g // ring

        def width(i, c):
            return min(CH, seen[i] - c * CH)

        def tiles(w):
            return [(t, min(P, w - t * P)) for t in range(-(-w // P))]

        def near(i, c):
            first = i * P - BACK
            a, b = max(first, c * CH, 0), min(first + BAND, c * CH + width(i, c))
            return (a - c * CH, a - first, b - a) if b > a else None

        def copies(act, turn, s):
            i = s % NT
            for c in range(chunks[i]):
                g = chunk(s, c)
                k, w = g % TR, width(i, c)
                act.wait_ge(s_pt[k], nth(turn, g, TR) + 1)
                if w >= P:
                    last = act.copy(PT[:, k, 0:w // P, :], pPT[:, k, 0:w // P, :])
                if w % P:
                    last = act.copy(PT[0:w % P, k, w // P, :], pPT[0:w % P, k, w // P, :])
                last.then_inc(s_ptc[k], 1)

        @block.tensor
        def _(pe):
            def scores(turn, s):
                b, i = divmod(s, NT)
                hd = turn * 2 + b
                if i == 0:
                    pe.wait_ge(s_split, hd * 6 + 6)
                    pe.wait_ge(s_cv[b], turn * 32 + 32)
                at = slice(i * P, (i + 1) * P)
                for c in range(chunks[i]):
                    g = chunk(s, c)
                    k = g % KR
                    w = width(i, c)
                    keys = slice(c * CH, c * CH + w)
                    pe.wait_ge(s_cp[k], nth(turn, g, KR))
                    pe.matmul(pS[:, k, 0:w], lhsT=qh[b][:, at], rhs=ks[b][:, keys], start=True, stop=False)
                    last = pe.matmul(pS[:, k, 0:w], lhsT=ql[b][0:HD, at], rhs=k2[b][0:HD, keys],
                                     start=False, stop=True)
                    if near(i, c):
                        to, frm, n = near(i, c)
                        for z in range(2):
                            last = pe.matmul(pS[:, k, to:to + n], lhsT=ident_r[:],
                                             rhs=bias[z][:, ds(hd, 1), frm:frm + n].rearrange("p a b -> p (a b)"),
                                             start=False, stop=True, skip_group_check=True)
                    last.then_inc(s_sc[k], 1)

            def turn_over(turn, s, c):
                i, g = s % NT, chunk(s, c)
                k = g % TR
                pe.wait_ge(s_ptc[k], nth(turn, g, TR))
                for t, n in tiles(width(i, c)):
                    last = pe.transpose(pPT[0:n, k, t, :], sc[:, s % 4, c * CH + t * P:c * CH + t * P + n], ident[:])
                last.then_inc(s_pt[k], 1)

            def add(turn, s, c):
                b, i = divmod(s, NT)
                g = chunk(s, c)
                k = g % TR
                pe.wait_ge(s_ptc[k], nth(turn, g, TR) + 1)
                for t, n in tiles(width(i, c)):
                    kt = c * 4 + t
                    last = pe.matmul(pO[:, s % 2, 0:HD + 1], lhsT=PT[0:n, k, t, :], rhs=vv[0:n, b, kt, :],
                                     start=(kt == 0), stop=(kt == i + 1))
                return last
            def values(turn, s):
                n = chunks[s % NT]
                pe.wait_ge(s_ex, turn * STEPS + s + 1)
                turn_over(turn, s, 0)
                for c in range(1, n):
                    turn_over(turn, s, c)
                    if c == 1:
                        pe.wait_ge(s_o[s % 2], nth(turn, s, 2, STEPS))
                    add(turn, s, c - 1)

            def last_values(turn, s):
                n = chunks[s % NT]
                if n == 1:
                    pe.wait_ge(s_o[s % 2], nth(turn, s, 2, STEPS))
                add(turn, s, n - 1).then_inc(s_pv[s % 2], 1)

            pe.wait_ge(s_const, NT + 2)
            pe.wait_ge(s_bias, 2 * H)
            with pe.Fori(0, H // 2) as turn:
                for s in range(STEPS + LAG):
                    if s >= LAG:
                        values(turn, s - LAG)
                    if s < STEPS:
                        scores(turn, s)
                    if s >= LAG:
                        last_values(turn, s - LAG)

        @block.vector
        def _(v):
            own_ = Tally(v, s_dve)

            def maxima(turn, s):
                b, i = divmod(s, NT)
                if s >= 4:
                    v.wait_ge(s_pv[s % 2], nth(turn, s - 4, 2, STEPS) + 1)
                n = chunks[i]
                for c in range(n):
                    g = chunk(s, c)
                    k, w = g % KR, width(i, c)
                    v.wait_ge(s_sc[k], nth(turn, g, KR) + 1)
                    v.sem_inc(s_tick, 1)
                    start = OFF[i] + i * NMETA + c * CH
                    v.tensor_tensor_reduce(sc[:, s % 4, c * CH:c * CH + w], pS[:, k, 0:w], chosen[:, start:start + w],
                                           1.0, 3.0 * NEG, ALU.add, ALU.max, accum_out=mxc[:, s % 2, c:c + 1]
                                           ).then_inc(s_cp[k], 1)
                for k in range(min(n, KR)):
                    g = chunk(s, n - 1 - k)
                    v.wait_ge(s_cp[g % KR], nth(turn, g, KR) + 1)
                own_.up(v.tensor_reduce(mx[:, s % 2:s % 2 + 1], mxc[:, s % 2, 0:n], AX.X, ALU.max))
                own_.settle()
                v.tensor_scalar(nm[:, s % 4:s % 4 + 1], mx[:, s % 2:s % 2 + 1], -0.125, None, ALU.mult
                                ).then_inc(s_nm, 1)

            def scale(turn, s):
                b, i = divmod(s, NT)
                v.wait_ge(s_pv[s % 2], nth(turn, s, 2, STEPS) + 1)
                own_.up(v.reciprocal(rd[:, s % 2:s % 2 + 1], pO[:, s % 2, HD:HD + 1]))
                if i == 0:
                    v.wait_ge(s_st, turn * 32)
                own_.settle()
                v.tensor_scalar(oh[:, b, i, :], pO[:, s % 2, 0:HD], rd[:, s % 2:s % 2 + 1], None, ALU.mult
                                ).then_inc(s_o[s % 2], 1)

            v.wait_ge(s_mk, 16 * NT)
            v.wait_ge(s_const, NT + 2)
            with v.Fori(0, H // 2) as turn:
                own_.enter(turn, 2 * STEPS)
                for s in range(STEPS + LAG):
                    if s < STEPS:
                        maxima(turn, s)
                    if s >= LAG:
                        scale(turn, s - LAG)
                own_.leave(H // 2)

        @block.scalar
        def _(act):
            def exps(turn, s):
                n = seen[s % NT]
                act.wait_ge(s_nm, turn * STEPS + s + 1)
                act.activation(sc[:, s % 4, 0:n], sc[:, s % 4, 0:n], ACT.Exp, bias=nm[:, s % 4:s % 4 + 1], scale=0.125
                               ).then_inc(s_ex, 1)

            with act.Fori(0, H // 2) as turn:
                for s in range(STEPS + LAG):
                    if s >= LAG:
                        copies(act, turn, s - LAG)
                    if 1 <= s <= STEPS:
                        exps(turn, s - 1)


SCRATCH_ROW = H * HD


def build_program(nc, x, c, positions, w_ada, b_ada, g_pre, w_in, b_fgate, sinks, w_out, g_post, meta_tokens,
                  rel_bias, lb_raw, w_in_2, kv_norm_g, w_uk, w_uv, hgrn_norm_g, w_out_2, ln_g, ln_b,
                  inv_freq, buckets, out):
    def scratch(name, shape, dt=F32):
        return nc.dram_tensor("scratch_" + name, shape, dt, kind="Internal").ap()

    HALF = SCRATCH_ROW
    X1 = scratch("x1", (S, D))
    used = []
    QK, R1 = scratch("qk", (2 * HALF, S)), scratch("r1", (S, R1_COLS))
    cum2 = scratch("cum", (2 * H, S))
    OA, OB = scratch("oa", (S, HALF)), scratch("ob", (S, HALF))
    with ExitStack() as first:
        gate_row = first.enter_context(nc.sbuf_tensor("gate_row", [P, D], F32))
        with ExitStack() as rows:
            hT = [rows.enter_context(nc.sbuf_tensor(n, [P, DC, S], F32R)) for n in ("hT_high", "hT_low")]
            stage_modulate(nc, used, x[0], c, w_ada, b_ada, g_pre, g_post, hT, gate_row)
            stage_project(nc, used, "p1_", hT, w_in,
                          [Job(R1_FIRST, R1_WIDTH, R1_GROUPS, False, R1), Job(0, P, 2 * HALF // P, True, QK)])
        stage_window(nc, used, R1, positions, inv_freq, b_fgate, sinks, cum2, OB)
        stage_forget(nc, used, QK, cum2, R1, OA)
        stage_out(nc, used, "o1_", (OA, OB), (R1[:, ZA:ZA + HALF], R1[:, ZB:ZB + HALF]), w_out, x[0], X1,
                  gate_row=gate_row)
    clear(nc, used)
    Q_A, C_KV, Q_IDX, K_IDX, W_IDX, Q_H, F_H, I_H, GATE_H = 0, 512, 640, 896, 960, 1476, 1988, 2500, 3012
    GATED = Q_H - W_IDX
    QAT, QI, KI = scratch("qa", (HALF, S)), scratch("qi", (IH * ID, S)), scratch("ki", (P, S))
    CK, CKm = scratch("ckv", (S, RANK)), scratch("ckv_meta", (NMETA, RANK))
    WX, GH = scratch("widx_gate", (S, GATED)), scratch("gate_h", (S, HALF))
    QH = scratch("qh", (HALF, S))
    FH, FHm = scratch("fh", (HALF, S)), scratch("fh_meta", (HALF, NMETA))
    IV, IVm = scratch("ih", (S, HALF)), scratch("ih_meta", (NMETA, HALF))
    RR, AA = scratch("rr", (S, HALF)), scratch("aa", (S, HALF))
    MK = scratch("mask", (P, OFF[NT]), BF16)
    KT, VE = scratch("keys", (HALF, E)), scratch("values", (E, HALF))
    BV = scratch("bias", (H, P, PITCH))
    with ExitStack() as rows:
        hT = [rows.enter_context(nc.sbuf_tensor(n, [P, DC, E], F32R)) for n in ("hT2_high", "hT2_low")]
        stage_turn(nc, used, X1, meta_tokens, hT)
        stage_project(nc, used, "p2_", hT, w_in_2, [
            Job(I_H, 256, 2, False, IV, meta=IVm),
            Job(C_KV, RANK, 1, False, CK, meta=CKm),
            Job(GATE_H, 256, 2, False, GH),
            Job(W_IDX, GATED // 2, 2, False, WX),
            Job(F_H, P, HALF // P, True, FH, meta=FHm),
            Job(Q_H, P, HALF // P, True, QH),
            Job(Q_A, P, HALF // P, True, QAT),
            Job(Q_IDX, P, 2, True, QI),
            Job(K_IDX, ID, 1, True, KI, twice=True)])
    stage_recur(nc, used, QH, FH, FHm, IV, IVm, lb_raw, hgrn_norm_g, RR)
    stage_select(nc, used, QI, KI, WX[:, 0:IH], MK)
    clear(nc, used)
    stage_lift(nc, used, CK, CKm, kv_norm_g, w_uk, w_uv, rel_bias, buckets, KT, VE, BV)
    stage_latent(nc, used, QAT, KT, VE, BV, MK, AA)
    stage_out(nc, used, "o2_", (AA, RR), (WX[:, IH:GATED], GH), w_out_2, X1, out[0], ln=(ln_g, ln_b))


INPUTS = ["x", "c", "positions", "w_ada", "b_ada", "g_pre", "w_in", "b_fgate", "sinks", "w_out", "g_post",
          "meta_tokens_2", "rel_bias_2", "hgrn_lb_raw_2", "w_in_2", "kv_norm_g_2", "w_uk_2", "w_uv_2",
          "hgrn_norm_g_2", "w_out_2", "ln_g_2", "ln_b_2"]


def kernel(**inputs):
    import numpy as _np
    import concourse.bacc as _bacc
    from concourse import mybir as _mybir
    from concourse.bass_utils import run_bass_kernel_spmd as _run

    nc = _bacc.Bacc("TRN2", target_bir_lowering=False, num_devices=1)
    arrays, args = {}, []

    def add(name, a):
        arrays[f"in_{name}_dram"] = a
        args.append(nc.dram_tensor(f"in_{name}_dram", a.shape, _mybir.dt.from_np(a.dtype), kind="ExternalInput").ap())

    for name in INPUTS:
        add(name, _np.ascontiguousarray(inputs[name]))
    half = HD // 2
    add("inv_freq", (10000.0 ** (-_np.arange(half, dtype=_np.float32) / half)).astype(_np.float32)[None])
    add("buckets", bucket_table())
    args.append(nc.dram_tensor("out_0_dram", (1, S, D), _mybir.dt.float32, kind="ExternalOutput").ap())
    build_program(nc, *args)
    r = _run(nc, [arrays], core_ids=[0])
    return r.results[0]["out_0_dram"]
```
